# Optimizing a Trainium2 kernel written in Bass

```python
import jax, jax.numpy as jnp
from jax import lax
import numpy as np

D_MODEL = 1024
BATCH = 1
SEQ = 256
DEPTH = 2

CHUNK = 64
MIX_DIM = D_MODEL
MLA_HEADS = 8
MLA_NOPE = 64
MLA_ROPE = 32
MLA_V = 64
Q_LORA = 384
KV_LORA = 256
Q_BLOCK = 128
ROPE_THETA = 10000.0
CA_HEADS = 8
CA_HEAD_DIM = 64
LEFT_CHUNKS = 8
REL_CLIP = 128
FFN_DIM = 3584
N_EXPERTS = 8
TOP_K = 2
EXPERT_BLOCK = 256
EPS = 1e-6
NEG_INF = -1e30

CA_DIM = CA_HEADS * CA_HEAD_DIM
IN_SPLITS = (Q_LORA, KV_LORA, MLA_ROPE, CA_DIM, CA_DIM, CA_DIM)
IN_DIM = sum(IN_SPLITS)
N_DENSE = (DEPTH + 1) // 2
N_MOE = DEPTH // 2

kernel_name = 'hybrid_mla_chunkattn_moe_encoder'

def rms_norm(x, g):
    xf = x.astype(jnp.float32)
    y = xf * lax.rsqrt(jnp.mean(xf * xf, axis=-1, keepdims=True) + EPS)
    return (y * g.astype(jnp.float32)).astype(x.dtype)

def rope_tables(seq, dim, dtype):
    inv = 1.0 / (ROPE_THETA ** (jnp.arange(0, dim, 2, dtype=jnp.float32) / dim))
    ang = jnp.arange(seq, dtype=jnp.float32)[:, None] * inv[None, :]
    return jnp.cos(ang).astype(dtype), jnp.sin(ang).astype(dtype)

def apply_rope(x, cos, sin):
    x1, x2 = jnp.split(x, 2, axis=-1)
    return jnp.concatenate([x1 * cos - x2 * sin, x1 * sin + x2 * cos], axis=-1)

def mla_attention(c_q, c_kv, k_r, q_norm, w_uq, kv_norm, w_ukv):
    B, S, _ = c_q.shape
    cos, sin = rope_tables(S, MLA_ROPE, c_q.dtype)
    q = (rms_norm(c_q, q_norm) @ w_uq).reshape(B, S, MLA_HEADS, MLA_NOPE + MLA_ROPE)
    q_nope = q[..., :MLA_NOPE]
    q_rope = apply_rope(q[..., MLA_NOPE:], cos[:, None, :], sin[:, None, :])
    kv = (rms_norm(c_kv, kv_norm) @ w_ukv).reshape(B, S, MLA_HEADS, MLA_NOPE + MLA_V)
    k_nope, v = kv[..., :MLA_NOPE], kv[..., MLA_NOPE:]
    k_rope = apply_rope(k_r, cos, sin)
    scale = (MLA_NOPE + MLA_ROPE) ** -0.5
    n_blk = S // Q_BLOCK
    k_chunk = jnp.arange(S) // CHUNK

    def to_blocks(t):
        return jnp.moveaxis(t.reshape(B, n_blk, Q_BLOCK, *t.shape[2:]), 1, 0)

    def one_block(args):
        qn, qr, start = args
        s = (jnp.einsum('bqhd,bkhd->bhqk', qn, k_nope)
             + jnp.einsum('bqhr,bkr->bhqk', qr, k_rope)).astype(jnp.float32) * scale
        q_chunk = (start + jnp.arange(Q_BLOCK)) // CHUNK
        mask = k_chunk[None, :] <= q_chunk[:, None]
        p = jax.nn.softmax(jnp.where(mask, s, NEG_INF), axis=-1).astype(v.dtype)
        return jnp.einsum('bhqk,bkhd->bqhd', p, v)

    out = lax.map(one_block, (to_blocks(q_nope), to_blocks(q_rope), jnp.arange(n_blk) * Q_BLOCK))
    return jnp.moveaxis(out, 0, 1).reshape(B, S, MLA_HEADS * MLA_V)

def chunk_attention(q, k, v, rel_bias):
    B, S, _ = q.shape
    n_chunks = S // CHUNK
    band = LEFT_CHUNKS + 1
    shp = (B, n_chunks, CHUNK, CA_HEADS, CA_HEAD_DIM)
    q, k, v = q.reshape(shp), k.reshape(shp), v.reshape(shp)
    pad = ((0, 0), (LEFT_CHUNKS, 0), (0, 0), (0, 0), (0, 0))
    band_idx = jnp.arange(n_chunks)[:, None] + jnp.arange(band)[None, :]
    band_shape = (B, n_chunks, band * CHUNK, CA_HEADS, CA_HEAD_DIM)
    kb = jnp.pad(k, pad)[:, band_idx].reshape(band_shape)
    vb = jnp.pad(v, pad)[:, band_idx].reshape(band_shape)
    valid = jnp.repeat(band_idx >= LEFT_CHUNKS, CHUNK, axis=1)
    q_pos = LEFT_CHUNKS * CHUNK + jnp.arange(CHUNK)
    k_pos = jnp.arange(band * CHUNK)
    rel = jnp.clip(q_pos[:, None] - k_pos[None, :], -REL_CLIP, REL_CLIP) + REL_CLIP
    bias = rel_bias[:, rel].astype(jnp.float32)
    s = jnp.einsum('bcqhd,bckhd->bchqk', q, kb).astype(jnp.float32) * (CA_HEAD_DIM ** -0.5) + bias
    s = jnp.where(valid[None, :, None, None, :], s, NEG_INF)
    p = jax.nn.softmax(s, axis=-1).astype(v.dtype)
    o = jnp.einsum('bchqk,bckhd->bcqhd', p, vb)
    return o.reshape(B, S, CA_DIM)

def swiglu(x, w1, w3, w2):
    return (jax.nn.silu(x @ w1) * (x @ w3)) @ w2

def moe_swiglu(x, w_router, w1, w3, w2):
    B, S, D = x.shape
    T = B * S
    n_assign = T * TOP_K
    xt = x.reshape(T, D)
    logits = (xt @ w_router).astype(jnp.float32)
    top_vals, top_idx = lax.top_k(logits, TOP_K)
    gates = jax.nn.softmax(top_vals, axis=-1)
    expert_ids = top_idx.reshape(-1).astype(jnp.int32)
    token_ids = (jnp.arange(n_assign) // TOP_K).astype(jnp.int32)
    gate_flat = gates.reshape(-1)
    order = jnp.argsort(expert_ids)
    sorted_e = expert_ids[order]
    counts = jnp.bincount(expert_ids, length=N_EXPERTS)
    padded = (counts + EXPERT_BLOCK - 1) // EXPERT_BLOCK * EXPERT_BLOCK
    starts = jnp.cumsum(counts) - counts
    pends = jnp.cumsum(padded)
    pstarts = pends - padded
    dest = pstarts[sorted_e] + (jnp.arange(n_assign) - starts[sorted_e])
    n_rows = n_assign + N_EXPERTS * EXPERT_BLOCK
    n_blocks = n_rows // EXPERT_BLOCK
    row_token = jnp.zeros((n_rows,), jnp.int32).at[dest].set(token_ids[order])
    row_gate = jnp.zeros((n_rows,), jnp.float32).at[dest].set(gate_flat[order])
    block_expert = jnp.minimum(
        jnp.searchsorted(pends, jnp.arange(n_blocks) * EXPERT_BLOCK, side='right'), N_EXPERTS - 1)
    xs = xt[row_token].reshape(n_blocks, EXPERT_BLOCK, D)

    def run(args):
        xb, e = args
        return swiglu(xb, w1[e], w3[e], w2[e])

    ys = lax.map(run, (xs, block_expert)).reshape(n_rows, D)
    ys = ys * row_gate[:, None].astype(ys.dtype)
    return jnp.zeros_like(xt).at[row_token].add(ys).reshape(B, S, D)

def setup_inputs(seed: int = 0) -> dict:
    key = jax.random.key(seed)
    ks = jax.random.split(key, 20)
    nrm = lambda k, shape, fan: jax.random.normal(k, shape, jnp.float32) * (fan ** -0.5)
    gain = lambda k, shape: 1.0 + 0.02 * jax.random.normal(k, shape, jnp.float32)
    return {
        'x': jax.random.normal(ks[0], (BATCH, SEQ, D_MODEL), jnp.float32),
        'attn_norm': gain(ks[1], (DEPTH, D_MODEL)),
        'w_in': nrm(ks[2], (DEPTH, D_MODEL, IN_DIM), D_MODEL),
        'q_norm': gain(ks[3], (DEPTH, Q_LORA)),
        'w_uq': nrm(ks[4], (DEPTH, Q_LORA, MLA_HEADS * (MLA_NOPE + MLA_ROPE)), Q_LORA),
        'kv_norm': gain(ks[5], (DEPTH, KV_LORA)),
        'w_ukv': nrm(ks[6], (DEPTH, KV_LORA, MLA_HEADS * (MLA_NOPE + MLA_V)), KV_LORA),
        'rel_bias': 0.1 * jax.random.normal(ks[7], (DEPTH, CA_HEADS, 2 * REL_CLIP + 1), jnp.float32),
        'w_out': nrm(ks[8], (DEPTH, MIX_DIM, D_MODEL), MIX_DIM),
        'ffn_norm': gain(ks[9], (DEPTH, D_MODEL)),
        'dense_w1': nrm(ks[10], (N_DENSE, D_MODEL, FFN_DIM), D_MODEL),
        'dense_w3': nrm(ks[11], (N_DENSE, D_MODEL, FFN_DIM), D_MODEL),
        'dense_w2': nrm(ks[12], (N_DENSE, FFN_DIM, D_MODEL), FFN_DIM),
        'w_router': nrm(ks[13], (N_MOE, D_MODEL, N_EXPERTS), D_MODEL),
        'moe_w1': nrm(ks[14], (N_MOE, N_EXPERTS, D_MODEL, FFN_DIM), D_MODEL),
        'moe_w3': nrm(ks[15], (N_MOE, N_EXPERTS, D_MODEL, FFN_DIM), D_MODEL),
        'moe_w2': nrm(ks[16], (N_MOE, N_EXPERTS, FFN_DIM, D_MODEL), FFN_DIM),
        'final_norm': gain(ks[17], (D_MODEL,)),
    }

def reference(x, attn_norm, w_in, q_norm, w_uq, kv_norm, w_ukv, rel_bias, w_out, ffn_norm,
              dense_w1, dense_w3, dense_w2, w_router, moe_w1, moe_w3, moe_w2, final_norm):
    split_points = [int(v) for v in np.cumsum(IN_SPLITS)[:-1]]
    for i in range(DEPTH):
        h = rms_norm(x, attn_norm[i])
        c_q, c_kv, k_r, q_b, k_b, v_b = jnp.split(h @ w_in[i], split_points, axis=-1)
        a = mla_attention(c_q, c_kv, k_r, q_norm[i], w_uq[i], kv_norm[i], w_ukv[i])
        b = chunk_attention(q_b, k_b, v_b, rel_bias[i])
        x = x + jnp.concatenate([a, b], axis=-1) @ w_out[i]
        h = rms_norm(x, ffn_norm[i])
        j = i // 2
        if i % 2 == 0:
            f = swiglu(h, dense_w1[j], dense_w3[j], dense_w2[j])
        else:
            f = moe_swiglu(h, w_router[j], moe_w1[j], moe_w3[j], moe_w2[j])
        x = x + f
    return rms_norm(x, final_norm)


_drawn_inputs = setup_inputs


def setup_inputs(seed=0):
    import zlib

    import numpy as np

    out = dict(_drawn_inputs(seed))
    spreads = {}
    factors = {'attn_norm': 4.894,
     'q_norm': 8.0,
     'kv_norm': 4.668,
     'rel_bias': 2.89,
     'final_norm': 8.228,
     'ffn_norm': 2.887}
    for name, (base, spread) in spreads.items():
        noise = np.random.default_rng([zlib.crc32(name.encode()), seed]).standard_normal(out[name].shape)
        drawn = base * np.exp(spread * noise) if base else spread * noise
        out[name] = __import__('jax').numpy.asarray(drawn.astype(out[name].dtype))
    for name, factor in factors.items():
        out[name] = (out[name] * factor).astype(out[name].dtype)
    return out
```

```python
from contextlib import ExitStack

import concourse.bass as bass
import numpy as np
from concourse import mybir

F32 = mybir.dt.float32
F32R = mybir.dt.float32r
I32 = mybir.dt.int32
ALU = mybir.AluOpType
ACT = mybir.ActivationFunctionType
AX = mybir.AxisListType

P = 128
D = 1024
SEQ = 256
TB = SEQ // P
DC = D // P
DEPTH = 2
Q_LORA, KV_LORA, ROPE = 384, 256, 32
LATENT = Q_LORA + KV_LORA
LC = LATENT // P
QC = Q_LORA // P
HEADS, HD, NOPE = 8, 64, 64
QK_MLA = NOPE + ROPE
CA = HEADS * HD
IN_DIM = LATENT + ROPE + 3 * CA
CA_Q, CA_K, CA_V = LATENT + ROPE, LATENT + ROPE + CA, LATENT + ROPE + 2 * CA
HALF = ROPE // 2
CHUNK = 64
REL = 128
FFN = 3584
EXPERTS = 8
EPS = 1e-6
NEG = -1e30

TILE = 2048
N_IN = 4
REST = IN_DIM - N_IN * 512
ATTN_TILES = 2 * N_IN + 1 + 2 + 1 + 4
UNIT = 512
UNITS = FFN // UNIT
UNIT_TILES = 6
FFN_TILES = UNIT_TILES * UNITS
RAW, HI, LO = 6, 3, 3
LEAD = 3
HEAD_STEPS = 2 * HEADS
SCORES = P + SEQ
NORMS = 5
PERIOD = 3 * P
PASS_SLOTS = P

C_ID, C_MASK, C_TRI, C_ONE, C_IOTA = 0, P, P + SCORES, 2 * P + SCORES, 3 * P + SCORES
C_COS = C_IOTA + P
C_SIN = C_COS + TB * HALF
C_ALL = C_SIN + TB * HALF

FIRST_TILE = {"attn0": 0, "ffn0": ATTN_TILES, "attn1": ATTN_TILES + FFN_TILES,
              "moe": 2 * ATTN_TILES + FFN_TILES}


def build(nc, t, out):
    with ExitStack() as ctx:
        def sb(name, shape, dt=F32):
            return ctx.enter_context(nc.sbuf_tensor(name, shape, dt))

        def sem(name):
            return ctx.enter_context(nc.semaphore(name))

        raw = sb("raw", [P, RAW, TILE])
        w_hi = sb("w_hi", [P, HI, TILE], F32R)
        w_lo = sb("w_lo", [P, LO, TILE], F32R)
        x = sb("x", [P, TB, D])
        xn = sb("xn", [P, TB, D])
        xT_hi = sb("xT_hi", [P, DC, SEQ], F32R)
        xT_lo = sb("xT_lo", [P, DC, SEQ], F32R)
        z = sb("z", [P, TB, IN_DIM])
        uT_hi = sb("uT_hi", [P, LC, SEQ], F32R)
        uT_lo = sb("uT_lo", [P, LC, SEQ], F32R)
        k_mla = sb("k_mla", [P, TB, HEADS, QK_MLA])
        v_mla = sb("v_mla", [P, TB, HEADS * HD])
        bias = sb("bias", [P, HEADS, SCORES])
        const = sb("const", [P, C_ALL])
        gain = sb("gain", [P, D])
        lat_gain = sb("lat_gain", [P, LATENT])
        qkT = sb("qkT", [P, 2, 2 * SEQ])
        s_sb = sb("s_sb", [P, 3, SCORES])
        pT = sb("pT", [P, 2, SCORES])
        rot = sb("rot", [P, 4, P])
        neg_max = sb("neg_max", [P, 3, TB])
        p_sum = sb("p_sum", [P, 3, TB])
        p_inv = sb("p_inv", [P, 3, TB])
        n_ss = sb("n_ss", [P, 4])
        n_ms = sb("n_ms", [P, 4])
        n_sd = sb("n_sd", [P, 4])
        n_inv = sb("n_inv", [P, 4])
        ext = sb("ext", [DEPTH * HEADS, PERIOD])
        wr = sb("wr", [P, DC, EXPERTS])
        wr_hi = sb("wr_hi", [P, DC, EXPERTS], F32R)
        wr_lo = sb("wr_lo", [P, DC, EXPERTS], F32R)
        rt = sb("rt", [P, 8, TB, EXPERTS])
        r1 = sb("r1", [P, 8, TB])
        chosen = sb("chosen", [P, TB, EXPERTS + 1])
        gates = sb("gates", [P, TB, EXPERTS + 1])
        pos = sb("pos", [P, TB, EXPERTS + 1])
        full = sb("full", [P, 2])
        full_i = sb("full_i", [P, 1], I32)
        ps = ctx.enter_context(nc.psum_tensor("ps", [P, 8, 512], F32))
        ext_dram = nc.dram_tensor("ext_dram", [DEPTH * HEADS, P * PERIOD], F32, kind="Internal").ap()

        ident = const[:, C_ID:C_ID + P]
        mask = const[:, C_MASK:C_MASK + SCORES]
        tri = const[:, C_TRI:C_TRI + P]
        ones = const[:, C_ONE:C_ONE + P]
        iota = const[:, C_IOTA:C_IOTA + P]
        cos = const[:, C_COS:C_SIN].rearrange("p (b j) -> p b j", b=TB)
        sin = const[:, C_SIN:C_ALL].rearrange("p (b j) -> p b j", b=TB)
        q_mla = xn[:, :, 0:HEADS * QK_MLA]
        z_flat = z[:, :, :].rearrange("p b n -> p (b n)")
        silu = z_flat[:, 0:2 * UNIT].rearrange("p (b n) -> p b n", b=TB)
        hid = z_flat[:, 2 * UNIT:4 * UNIT].rearrange("p (b n) -> p b n", b=TB)
        y_sb = z_flat[:, 4 * UNIT:4 * UNIT + D]
        pick = z_flat[:, 6 * UNIT:6 * UNIT + SEQ].rearrange("p (b s) -> p b s", b=TB)
        pickT = z_flat[:, 6 * UNIT + SEQ:6 * UNIT + 2 * SEQ]

        landed = [sem(f"landed{i}") for i in range(RAW)]
        hi_ready = sem("hi_ready")
        lo_ready = sem("lo_ready")
        used = sem("used")
        const_in = sem("const_in")
        x_in = sem("x_in")
        gain_in = sem("gain_in")
        lat_gain_in = sem("lat_gain_in")
        rel_in = sem("rel_in")
        router_in = sem("router_in")
        ext_done = sem("ext_done")
        ext_out = sem("ext_out")
        bias_in = sem("bias_in")
        bias_ready = sem("bias_ready")
        x_updated = sem("x_updated")
        norm_ss = sem("norm_ss")
        norm_ms = sem("norm_ms")
        norm_sd = sem("norm_sd")
        xn_ready = sem("xn_ready")
        lat_ss = sem("lat_ss")
        lat_ms = sem("lat_ms")
        lat_sd = sem("lat_sd")
        lat_ready = sem("lat_ready")
        tr_done = sem("tr_done")
        tr_hi = sem("tr_hi")
        tr_lo = sem("tr_lo")
        z_out = sem("z_out")
        lt_done = sem("lt_done")
        lt_hi = sem("lt_hi")
        lt_lo = sem("lt_lo")
        q_out = sem("q_out")
        kv_out = sem("kv_out")
        k_roped = sem("k_roped")
        q_roped = sem("q_roped")
        qk_done = sem("qk_done")
        qk_out = sem("qk_out")
        sc_done = sem("sc_done")
        sc_out = sem("sc_out")
        max_done = sem("max_done")
        exp_done = sem("exp_done")
        p_ready = sem("p_ready")
        pT_done = sem("pT_done")
        pT_out = sem("pT_out")
        o_done = sem("o_done")
        o_hi = sem("o_hi")
        o_lo = sem("o_lo")
        silu_done = sem("silu_done")
        hid_done = sem("hid_done")
        ht_done = sem("ht_done")
        ht_hi = sem("ht_hi")
        ht_lo = sem("ht_lo")
        rw_hi = sem("rw_hi")
        rw_lo = sem("rw_lo")
        logit_done = sem("logit_done")
        gate_exp_in = sem("gate_exp_in")
        gate_exp = sem("gate_exp")
        chosen_done = sem("chosen_done")
        pos_done = sem("pos_done")
        routed = sem("routed")
        pick_done = sem("pick_done")
        ga_done = sem("ga_done")
        ga_hi = sem("ga_hi")
        ga_lo = sem("ga_lo")
        st_done = sem("st_done")
        st_out = sem("st_out")
        y_out = sem("y_out")
        sct_done = sem("sct_done")
        x_acc = sem("x_acc")
        dve_step = sem("dve_step")
        out_stored = sem("out_stored")

        def width(n):
            for base in (FIRST_TILE["attn0"], FIRST_TILE["attn1"]):
                k = n - base
                if 0 <= k < ATTN_TILES:
                    if k == 2 * N_IN:
                        return DC * REST
                    if k in (2 * N_IN + 1, 2 * N_IN + 2):
                        return QC * Q_LORA
            return TILE

        def hi_of(n, cols):
            w = width(n)
            return w_hi[:, n % HI, 0:w].rearrange("p (k n) -> p k n", n=cols)

        def lo_of(n, cols):
            w = width(n)
            return w_lo[:, n % LO, 0:w].rearrange("p (k n) -> p k n", n=cols)

        def load(eng, n, step, src):
            if n >= RAW:
                eng.wait_ge(lo_ready, n - RAW + 1 + UNIT_TILES * step)
            shape = src.shape
            dst = raw[:, n % RAW, 0:width(n)].rearrange("p (k n) -> p k n", n=shape[2])
            eng.dma_start(dst, src).then_inc(landed[n % RAW], 16)

        def round_hi(act, n, step=0):
            act.wait_ge(landed[n % RAW], 16 * (n // RAW + 1) + 16 * (UNIT_TILES // RAW) * step)
            if n >= HI:
                act.wait_ge(used, n - HI + 1 + UNIT_TILES * step)
            w = width(n)
            nc.scalar.activation(w_hi[:, n % HI, 0:w], raw[:, n % RAW, 0:w], ACT.Copy).then_inc(hi_ready, 1)

        def split_lo(dve, n, step=0):
            dve.wait_ge(hi_ready, n + 1 + UNIT_TILES * step)
            if n >= LO:
                dve.wait_ge(used, n - LO + 1 + UNIT_TILES * step)
            w = width(n)
            nc.vector.tensor_tensor(w_lo[:, n % LO, 0:w], raw[:, n % RAW, 0:w],
                                    w_hi[:, n % HI, 0:w].bitcast(F32), ALU.subtract).then_inc(lo_ready, 1)

        def multiplied(eng, n, step=0):
            eng.wait_ge(used, n + 1 + UNIT_TILES * step)

        def product(out_ap, x_hi, x_lo, y_hi, y_lo, start, stop):
            nc.tensor.matmul(out_ap, x_hi, y_hi, start=start, stop=False)
            nc.tensor.matmul(out_ap, x_hi, y_lo, start=False, stop=False)
            return nc.tensor.matmul(out_ap, x_lo, y_hi, start=False, stop=stop)

        def bank(b, n=512):
            return ps[:, b, 0:n]

        tok = [slice(b * P, (b + 1) * P) for b in range(TB)]
        HEAD_ORDER = [(True, h) for h in range(HEADS)] + [(False, h) for h in range(HEADS)]

        def head_dims(ca):
            return HD if ca else QK_MLA

        EXPERT_STEPS = UNITS
        MOE = FIRST_TILE["moe"]
        DENSE_UNITS = TB * UNITS

        def passes(emit, eng, p):
            it0 = p * EXPERTS
            emit(eng, it0, True, False)
            with eng.Fori(it0 + 1, it0 + EXPERTS - 1) as it:
                emit(eng, it, False, False)
            emit(eng, it0 + EXPERTS - 1, False, True)

        block = ctx.enter_context(nc.Block())

        @block.sync
        def _(sp):
            sp.dma_start(const[:, :], t["const"]).then_inc(const_in, 16)
            sp.dma_start(x[:, :, :], t["x"].rearrange("a (b p) d -> p (a b) d", p=P)).then_inc(x_in, 16)

            def attn_tiles(layer):
                n = FIRST_TILE[f"attn{layer}"]
                w_in = t["w_in"][layer].rearrange("(k p) n -> p k n", p=P)
                for g in range(N_IN):
                    for half in range(2):
                        load(sp, n, 0, w_in[:, 4 * half:4 * half + 4, 512 * g:512 * g + 512])
                        n += 1
                load(sp, n, 0, w_in[:, :, 512 * N_IN:IN_DIM])
                w_uq = t["w_uq"][layer].rearrange("(k p) n -> p k n", p=P)
                for j in range(2):
                    load(sp, n + 1 + j, 0, w_uq[:, :, Q_LORA * j:Q_LORA * (j + 1)])
                load(sp, n + 3, 0, t["w_ukv"][layer].rearrange("(k p) n -> p k n", p=P))
                w_out = t["w_out"][layer].rearrange("(k p) n -> p k n", p=P)
                for g in range(2):
                    for half in range(2):
                        load(sp, n + 4 + 2 * g + half, 0, w_out[:, 4 * half:4 * half + 4, 512 * g:512 * g + 512])

            def up_tiles(n, step, w, f):
                w = w.rearrange("(k p) n -> p k n", p=P)
                for half in range(2):
                    load(sp, n + half, step, w[:, 4 * half:4 * half + 4, bass.ds(f * UNIT, UNIT)])

            def down_tiles(n, step, w, f):
                w = w.rearrange("(u k p) n -> u p k n", p=P, k=4)
                for half in range(2):
                    src = w[bass.ds(f, 1), :, 2 * half:2 * half + 2, :]
                    load(sp, n + half, step, src.rearrange("u p k n -> p (u k) n"))

            def ffn_tiles(n, step, w1, w3, w2):
                up_tiles(n, step, w1, 0)
                up_tiles(n + 2, step, w3, 0)
                with sp.Fori(0, UNITS - 1) as f:
                    up_tiles(n + 4, step + f, w1, f + 1)
                    up_tiles(n + 6, step + f, w3, f + 1)
                    down_tiles(n + 8, step + f, w2, f)
                down_tiles(n + 4, step + UNITS - 1, w2, UNITS - 1)

            def expert_tiles(it, e):
                def of(name):
                    return t[name][0, bass.ds(e, 1)].rearrange("e a b -> (e a) b")
                ffn_tiles(MOE, EXPERT_STEPS * it, of("moe_w1"), of("moe_w3"), of("moe_w2"))

            attn_tiles(0)
            ffn_tiles(FIRST_TILE["ffn0"], 0, t["dense_w1"][0], t["dense_w3"][0], t["dense_w2"][0])
            attn_tiles(1)
            with sp.Fori(0, EXPERTS) as e:
                expert_tiles(e, e)
            sp.wait_ge(routed, 1)
            more = sp.value_load(full_i[0:1, 0:1], min_val=0, max_val=1)
            with sp.If(more == 1):
                with sp.Fori(0, EXPERTS) as e:
                    expert_tiles(e + EXPERTS, e)
                sp.wait_ge(x_acc, 2 * 4 * EXPERTS)
            for b in range(TB):
                sp.wait_ge(xn_ready, 2 * NORMS - 1 + b)
                sp.dma_start(out.rearrange("a (b p) d -> p (a b) d", p=P)[:, b, :], xn[:, b, :]).then_inc(out_stored, 16)
            sp.wait_ge(out_stored, 16 * TB)

        @block.gpsimd
        def _(pool):
            def load_gain(k):
                src = [t["attn_norm"][0:1], t["ffn_norm"][0:1], t["attn_norm"][1:2], t["ffn_norm"][1:2], t["final_norm"]][k]
                if k:
                    pool.wait_ge(xn_ready, 2 * k)
                pool.dma_start(gain[:, :], src.to_broadcast([P, D])).then_inc(gain_in, 16)

            def load_lat_gain(layer):
                if layer:
                    pool.wait_ge(lat_ready, 4 * layer)
                pool.dma_start(lat_gain[:, 0:Q_LORA], t["q_norm"][layer:layer + 1].to_broadcast([P, Q_LORA])).then_inc(lat_gain_in, 16)
                pool.dma_start(lat_gain[:, Q_LORA:LATENT], t["kv_norm"][layer:layer + 1].to_broadcast([P, KV_LORA])).then_inc(lat_gain_in, 16)

            def load_bias(layer):
                if layer:
                    pool.wait_ge(sc_out, HEAD_STEPS * layer)
                for first, base, n in ((0, 2 * REL - 1, P), (P, REL - 1, SEQ)):
                    e = ext_dram[layer * HEADS:(layer + 1) * HEADS, base:base + 1]
                    src = bass.AP(e.tensor, e.offset, [[PERIOD - 1, P], [P * PERIOD, HEADS], [1, n]])
                    pool.dma_start(bias[:, :, first:first + n], src).then_inc(bias_in, 16)
                pool.wait_ge(bias_in, 32 * (layer + 1))
                for diagonal in (0, 2 * P):
                    nc.gpsimd.memset(bias[0:CHUNK, :, diagonal + CHUNK:diagonal + P], NEG).then_inc(bias_ready, 1)

            load_gain(0)
            load_lat_gain(0)
            pool.dma_start(ext[:, REL - 1:PERIOD], t["rel_rev"][:, 0:2 * REL + 1]).then_inc(rel_in, 16)
            pool.dma_start(wr[:, :, :], t["w_router"][0].rearrange("(k p) e -> p k e", p=P)).then_inc(router_in, 16)
            pool.wait_ge(rel_in, 16)
            nc.gpsimd.tensor_copy(ext[:, 0:REL - 1], ext[:, REL - 1:REL].to_broadcast([DEPTH * HEADS, REL - 1])).then_inc(ext_done, 1)
            pool.wait_ge(ext_done, 1)
            rows = bass.AP(ext[:, :].tensor, ext[:, :].offset, [ext[:, :].ap[0], [0, P], [1, PERIOD]])
            pool.dma_start(ext_dram.rearrange("h (r d) -> h r d", r=P), rows).then_inc(ext_out, 16)
            pool.wait_ge(ext_out, 16)
            load_bias(0)
            load_gain(1)
            load_gain(2)
            load_lat_gain(1)
            load_bias(1)
            load_gain(3)
            load_gain(4)

        @block.scalar
        def _(act):
            def norm(k):
                if k == 0:
                    act.wait_ge(x_in, 16)
                else:
                    act.wait_ge(x_updated, k)
                for b in range(TB):
                    nc.scalar.activation(xn[:, b, :], x[:, b, :], ACT.Square,
                                         accum_out=n_ss[:, b:b + 1]).then_inc(norm_ss, 1)
                act.wait_ge(norm_ms, k + 1)
                nc.scalar.activation(n_sd[:, 0:TB], n_ms[:, 0:TB], ACT.Sqrt).then_inc(norm_sd, 1)

            def transposed_hi(k):
                for g in range(4):
                    act.wait_ge(tr_done, 4 * k + g + 1)
                    nc.scalar.activation(xT_hi[:, 2 * g:2 * g + 2, :], bank(g), ACT.Copy).then_inc(tr_hi, 1)

            def attention(layer):
                n0 = FIRST_TILE[f"attn{layer}"]
                norm(2 * layer)
                transposed_hi(2 * layer)

                def z_copy(g):
                    multiplied(act, n0 + min(2 * g + 1, 2 * N_IN))
                    for b in range(TB):
                        w = 512 if g < N_IN else REST
                        nc.scalar.activation(z[:, b, 512 * g:512 * g + w], bank(4 + 2 * (g % 2) + b, w),
                                             ACT.Copy).then_inc(z_out, 1)

                n = n0 + LEAD
                for g in range(N_IN + 1):
                    for half in range(2 if g < N_IN else 1):
                        round_hi(act, n)
                        n += 1
                    z_copy(g)
                    if g == 1:
                        act.wait_ge(z_out, 10 * layer + 4)
                        for b in range(TB):
                            for j, (a, c) in enumerate(((0, Q_LORA), (Q_LORA, LATENT))):
                                nc.scalar.activation(xn[:, b, a:c], z[:, b, a:c], ACT.Square,
                                                     accum_out=n_ss[:, 2 * j + b:2 * j + b + 1]).then_inc(lat_ss, 1)
                    if g == 2:
                        act.wait_ge(lat_ms, layer + 1)
                        nc.scalar.activation(n_sd[:, 0:4], n_ms[:, 0:4], ACT.Sqrt).then_inc(lat_sd, 1)
                for g in range(3):
                    act.wait_ge(lt_done, 3 * layer + g + 1)
                    m = min(2, LC - 2 * g)
                    nc.scalar.activation(uT_hi[:, 2 * g:2 * g + m, :], bank(g, m * SEQ), ACT.Copy).then_inc(lt_hi, 1)
                for j in range(2):
                    multiplied(act, n0 + 2 * N_IN + 1 + j)
                    for b in range(TB):
                        nc.scalar.activation(q_mla[:, b, Q_LORA * j:Q_LORA * (j + 1)], bank(4 + 2 * j + b, Q_LORA),
                                             ACT.Copy).then_inc(q_out, 1)
                    round_hi(act, n)
                    n += 1
                multiplied(act, n0 + 2 * N_IN + 3)
                for g in range(2):
                    for b in range(TB):
                        kv = bank(2 * g + b).rearrange("p (h c) -> p h c", c=2 * HD)
                        nc.scalar.activation(k_mla[:, b, 4 * g:4 * g + 4, 0:NOPE], kv[:, :, 0:HD], ACT.Copy)
                        v = v_mla[:, b, :].rearrange("p (h c) -> p h c", c=HD)
                        nc.scalar.activation(v[:, 4 * g:4 * g + 4, :], kv[:, :, HD:2 * HD], ACT.Copy).then_inc(kv_out, 1)
                round_hi(act, n)
                n += 1
                for s in range(HEAD_STEPS + 4):
                    i = HEAD_STEPS * layer + s
                    if s < HEAD_STEPS:
                        act.wait_ge(qk_done, i + 1)
                        if i >= 2:
                            act.wait_ge(sc_done, i - 1)
                        d = head_dims(HEAD_ORDER[s][0])
                        nc.scalar.activation(qkT[0:d, i % 2, :], ps[0:d, i % 2, :], ACT.Copy).then_inc(qk_out, 1)
                    if 2 <= s < HEAD_STEPS + 2:
                        j = i - 2
                        act.wait_ge(max_done, j + 1)
                        for b, (a, c) in enumerate(((0, P), (P, SCORES))):
                            ins = nc.scalar.activation(s_sb[:, j % 3, a:c], s_sb[:, j % 3, a:c], ACT.Exp,
                                                       bias=neg_max[:, j % 3, b:b + 1], accum_out=p_sum[:, j % 3, b:b + 1])
                        ins.then_inc(exp_done, 1)
                    if 3 <= s < HEAD_STEPS + 3:
                        j = i - 3
                        act.wait_ge(pT_done, j + 1)
                        if j >= 2:
                            act.wait_ge(o_done, j - 1)
                        nc.scalar.activation(pT[:, j % 2, :], bank(4 + j % 2, SCORES), ACT.Copy).then_inc(pT_out, 1)
                    if s >= 4:
                        j = i - 4
                        act.wait_ge(o_done, j + 1)
                        ca, h = HEAD_ORDER[s - 4]
                        r = slice(HD * (h % 2), HD * (h % 2) + HD)
                        c = (HEADS * ca + h) // 2
                        nc.scalar.activation(xT_hi[r, c, :], ps[r, 6 + j % 2, 0:SEQ], ACT.Copy).then_inc(o_hi, 1)
                for _ in range(4):
                    round_hi(act, n)
                    n += 1

            def ffn(n, step, u0, blocks, extra=None, cut=False, xtra_end=None):
                def silu_of(f, st=None):
                    multiplied(act, n + 1 if st is None else n + 5, step if st is None else st)
                    for b in range(blocks):
                        act.wait_ge(hid_done, u0 + blocks * f + b + 1 - blocks) if not _is_zero(u0, f) else None
                        nc.scalar.activation(silu[:, b, :], bank(b), ACT.Silu).then_inc(silu_done, 1)

                def hidden_hi(f):
                    for b in range(blocks):
                        act.wait_ge(ht_done, u0 + blocks * f + b + 1)
                        nc.scalar.activation(uT_hi[:, 0:4, tok[b]],
                                             bank(2 + b).rearrange("p (k s) -> p k s", s=P), ACT.Copy).then_inc(ht_hi, 1)

                round_hi(act, n + 3, step)
                silu_of(0)
                for j in (4, 5, 6):
                    round_hi(act, n + j, step)
                if extra:
                    extra()
                hidden_hi(0)

                def unit(f, st, tail):
                    round_hi(act, n + 7, st)
                    round_hi(act, n + 8, st)
                    silu_of(f, st)
                    for j in (9, 10, 11, 12)[:4 - tail]:
                        round_hi(act, n + j, st)
                    hidden_hi(f)

                with act.Fori(1, UNITS - 1) as f:
                    unit(f, step + f - 1, 0)
                unit(UNITS - 1, step + UNITS - 2, 1 if cut else 0)
                if xtra_end:
                    xtra_end()
                if not cut:
                    round_hi(act, n + 7, step + UNITS - 1)
                    round_hi(act, n + 8, step + UNITS - 1)

            def gathered_hi(it):
                for g in range(2):
                    act.wait_ge(ga_done, 2 * it + g + 1)
                    nc.scalar.activation(xT_hi[:, 4 * g:4 * g + 4, 0:P], bank(1 + 2 * g).rearrange("p (k s) -> p k s", s=P),
                                         ACT.Copy).then_inc(ga_hi, 1)

            def expert(act, it, first, last):
                def pick_copy():
                    if not first:
                        act.wait_ge(sct_done, 4 * it)
                    act.wait_ge(st_done, it + 1)
                    nc.scalar.activation(pickT, ps[:, 6, 0:SEQ], ACT.Copy).then_inc(st_out, 1)

                def gather_next():
                    if not last:
                        gathered_hi(it + 1)

                ffn(MOE, EXPERT_STEPS * it, DENSE_UNITS + UNITS * it, 1, extra=pick_copy, cut=last, xtra_end=gather_next)
                multiplied(act, MOE + 5, EXPERT_STEPS * it + UNITS - 1)
                if not first:
                    act.wait_ge(sct_done, 4 * it)
                for g in range(2):
                    nc.scalar.activation(y_sb[:, 512 * g:512 * g + 512], bank(4 + g), ACT.Copy).then_inc(y_out, 1)

            for n in range(LEAD):
                round_hi(act, n)
            act.wait_ge(const_in, 16)
            attention(0)
            norm(1)
            transposed_hi(1)
            ffn(FIRST_TILE["ffn0"], 0, 0, TB)
            attention(1)
            act.wait_ge(router_in, 16)
            nc.scalar.activation(wr_hi[:, :, :], wr[:, :, :], ACT.Copy).then_inc(rw_hi, 1)
            norm(3)
            transposed_hi(3)
            act.wait_ge(gate_exp_in, 1)
            nc.scalar.activation(r1[:, 5, :], r1[:, 4, :], ACT.Exp).then_inc(gate_exp, 1)
            gathered_hi(0)
            passes(expert, act, 0)
            act.wait_ge(routed, 1)
            more = act.value_load(full_i[0:1, 0:1], min_val=0, max_val=1)
            with act.If(more == 1):
                for n in range(LEAD):
                    round_hi(act, MOE + n, EXPERT_STEPS * EXPERTS)
                gathered_hi(EXPERTS)
                passes(expert, act, 1)
            norm(4)

        @block.vector
        def _(dve):
            chain = [0]

            def link(ins):
                chain[0] += 1
                ins.then_inc(dve_step, 1)
                dve.wait_ge(dve_step, chain[0])

            def norm(k):
                dve.wait_ge(norm_ss, TB * (k + 1))
                nc.vector.tensor_scalar(n_ms[:, 0:TB], n_ss[:, 0:TB], 1.0 / D, EPS, ALU.mult, ALU.add).then_inc(norm_ms, 1)
                dve.wait_ge(norm_sd, k + 1)
                link(nc.vector.reciprocal(n_inv[:, 0:TB], n_sd[:, 0:TB]))
                dve.wait_ge(gain_in, 16 * (k + 1))
                for b in range(TB):
                    nc.vector.scalar_tensor_tensor(xn[:, b, :], x[:, b, :], n_inv[:, b:b + 1], gain[:, :],
                                                   ALU.mult, ALU.mult).then_inc(xn_ready, 1)

            def transposed_lo(k):
                for g in range(4):
                    dve.wait_ge(tr_hi, 4 * k + g + 1)
                    nc.vector.tensor_tensor(xT_lo[:, 2 * g:2 * g + 2, :], bank(g).rearrange("p (k s) -> p k s", s=SEQ),
                                            xT_hi[:, 2 * g:2 * g + 2, :].bitcast(F32), ALU.subtract).then_inc(tr_lo, 1)

            def rotate(v, shape, out1, out2, done):
                v1, v2 = v[..., 0:HALF], v[..., HALF:ROPE]
                m = int(np.prod(shape))
                c, s = cos, sin
                if len(shape) == 3:
                    c = bass.AP(cos.tensor, cos.offset, [cos.ap[0], cos.ap[1], [0, shape[1]], cos.ap[2]])
                    s = bass.AP(sin.tensor, sin.offset, [sin.ap[0], sin.ap[1], [0, shape[1]], sin.ap[2]])
                    parts = [rot[:, i, 0:m].rearrange("p (b h j) -> p b h j", b=shape[0], h=shape[1]) for i in range(4)]
                else:
                    parts = [rot[:, i, 0:m].rearrange("p (b j) -> p b j", b=shape[0]) for i in range(4)]
                for i, (a, w) in enumerate(((v1, c), (v2, s), (v1, s), (v2, c))):
                    ins = nc.vector.tensor_tensor(parts[i], a, w, ALU.mult)
                link(ins)
                nc.vector.tensor_tensor(out1, parts[0], parts[1], ALU.subtract)
                ins = nc.vector.tensor_tensor(out2, parts[2], parts[3], ALU.add)
                if done is not None:
                    ins.then_inc(done, 1)
                else:
                    link(ins)

            def attention(layer):
                n0 = FIRST_TILE[f"attn{layer}"]
                n = n0 + LEAD
                norm(2 * layer)
                transposed_lo(2 * layer)
                for g in range(N_IN + 1):
                    for half in range(2 if g < N_IN else 1):
                        split_lo(dve, n)
                        n += 1
                    if g == 1:
                        dve.wait_ge(lat_ss, 4 * (layer + 1))
                        nc.vector.tensor_scalar(n_ms[:, 0:2], n_ss[:, 0:2], 1.0 / Q_LORA, EPS, ALU.mult, ALU.add)
                        nc.vector.tensor_scalar(n_ms[:, 2:4], n_ss[:, 2:4], 1.0 / KV_LORA, EPS, ALU.mult, ALU.add).then_inc(lat_ms, 1)
                        k_r = z[:, :, LATENT:LATENT + ROPE]
                        rotate(k_r, (TB, HALF), k_r[..., 0:HALF], k_r[..., HALF:ROPE], None)
                        for b in range(TB):
                            nc.vector.tensor_copy(k_mla[:, b, :, NOPE:QK_MLA],
                                                  z[:, b:b + 1, LATENT:LATENT + ROPE].to_broadcast([P, HEADS, ROPE])).then_inc(k_roped, 1)
                    if g == 2:
                        dve.wait_ge(lat_sd, layer + 1)
                        link(nc.vector.reciprocal(n_inv[:, 0:4], n_sd[:, 0:4]))
                        dve.wait_ge(lat_gain_in, 32 * (layer + 1))
                        for b in range(TB):
                            for j, (a, c) in enumerate(((0, Q_LORA), (Q_LORA, LATENT))):
                                nc.vector.scalar_tensor_tensor(z[:, b, a:c], z[:, b, a:c], n_inv[:, 2 * j + b:2 * j + b + 1],
                                                               lat_gain[:, a:c], ALU.mult, ALU.mult).then_inc(lat_ready, 1)
                for g in range(3):
                    dve.wait_ge(lt_hi, 3 * layer + g + 1)
                    m = min(2, LC - 2 * g)
                    nc.vector.tensor_tensor(uT_lo[:, 2 * g:2 * g + m, :], bank(g, m * SEQ).rearrange("p (k s) -> p k s", s=SEQ),
                                            uT_hi[:, 2 * g:2 * g + m, :].bitcast(F32), ALU.subtract).then_inc(lt_lo, 1)
                for j in range(2):
                    split_lo(dve, n)
                    n += 1
                dve.wait_ge(q_out, 4 * layer + 4)
                for b in range(TB):
                    q = q_mla[:, b, :].rearrange("p (h c) -> p h c", c=QK_MLA)[:, :, NOPE:QK_MLA]
                    v1, v2 = q[:, :, 0:HALF], q[:, :, HALF:ROPE]
                    cb = cos[:, b:b + 1, :].to_broadcast([P, HEADS, HALF])
                    sb_ = sin[:, b:b + 1, :].to_broadcast([P, HEADS, HALF])
                    parts = [rot[:, i, :].rearrange("p (h j) -> p h j", h=HEADS) for i in range(4)]
                    for i, (a, w) in enumerate(((v1, cb), (v2, sb_), (v1, sb_), (v2, cb))):
                        ins = nc.vector.tensor_tensor(parts[i], a, w, ALU.mult)
                    link(ins)
                    nc.vector.tensor_tensor(v1, parts[0], parts[1], ALU.subtract)
                    ins = nc.vector.tensor_tensor(v2, parts[2], parts[3], ALU.add)
                    ins.then_inc(q_roped, 1)
                    dve.wait_ge(q_roped, 2 * layer + b + 1)
                split_lo(dve, n)
                n += 1
                dve.wait_ge(bias_ready, 2 * (layer + 1))
                for s in range(1, HEAD_STEPS + 4):
                    i = HEAD_STEPS * layer + s
                    if s < HEAD_STEPS + 1:
                        j = i - 1
                        ca, h = HEAD_ORDER[s - 1]
                        dve.wait_ge(sc_done, j + 1)
                        if j >= 3:
                            dve.wait_ge(pT_done, j - 2)
                        nc.vector.scalar_tensor_tensor(s_sb[:, j % 3, :], bank(2 + j % 2, SCORES), head_dims(ca) ** -0.5,
                                                       bias[:, h, :] if ca else mask, ALU.mult, ALU.add).then_inc(sc_out, 1)
                        dve.wait_ge(sc_out, j + 1)
                        for b, (a, c) in enumerate(((0, P), (P, SCORES))):
                            ins = nc.vector.tensor_reduce(neg_max[:, j % 3, b:b + 1], s_sb[:, j % 3, a:c], AX.X, ALU.max, negate=True)
                        ins.then_inc(max_done, 1)
                    if 2 <= s < HEAD_STEPS + 2:
                        j = i - 2
                        dve.wait_ge(exp_done, j + 1)
                        link(nc.vector.reciprocal(p_inv[:, j % 3, :], p_sum[:, j % 3, :]))
                        for b, (a, c) in enumerate(((0, P), (P, SCORES))):
                            ins = nc.vector.tensor_scalar(s_sb[:, j % 3, a:c], s_sb[:, j % 3, a:c], p_inv[:, j % 3, b:b + 1], None, ALU.mult)
                        ins.then_inc(p_ready, 1)
                    if s >= 4:
                        j = i - 4
                        dve.wait_ge(o_hi, j + 1)
                        ca, h = HEAD_ORDER[s - 4]
                        r = slice(HD * (h % 2), HD * (h % 2) + HD)
                        c = (HEADS * ca + h) // 2
                        nc.vector.tensor_tensor(xT_lo[r, c, :], ps[r, 6 + j % 2, 0:SEQ], xT_hi[r, c, :].bitcast(F32),
                                                ALU.subtract).then_inc(o_lo, 1)
                for k in range(4):
                    split_lo(dve, n)
                    n += 1
                    if k % 2:
                        continue
                add_to_x((n0 + ATTN_TILES - 3, n0 + ATTN_TILES - 1), 0)

            def add_to_x(tiles, first_bank):
                for g in range(2):
                    multiplied(dve, tiles[g])
                    for b in range(TB):
                        cols = slice(512 * g, 512 * g + 512)
                        last = g == 1 and b == TB - 1
                        nc.vector.tensor_tensor(x[:, b, cols], bank(first_bank + 2 * g + b), x[:, b, cols],
                                                ALU.add).then_inc(x_updated if last else dve_step, 1)
                        if not last:
                            chain[0] += 1

            def ffn(n, step, u0, blocks, extra=None, cut=False, xtra_end=None, mid=None):
                def hidden(f, st=None):
                    multiplied(dve, n + 3 if st is None else n + 7, step if st is None else st)
                    for b in range(blocks):
                        dve.wait_ge(silu_done, u0 + blocks * f + b + 1)
                        if not _is_zero(u0, f):
                            dve.wait_ge(ht_done, u0 + blocks * f + b + 1 - blocks)
                        nc.vector.tensor_tensor(hid[:, b, :], bank(2 + b), silu[:, b, :], ALU.mult).then_inc(hid_done, 1)

                def hidden_lo(f):
                    for b in range(blocks):
                        dve.wait_ge(ht_hi, u0 + blocks * f + b + 1)
                        nc.vector.tensor_tensor(uT_lo[:, 0:4, tok[b]], bank(2 + b).rearrange("p (k s) -> p k s", s=P),
                                                uT_hi[:, 0:4, tok[b]].bitcast(F32), ALU.subtract).then_inc(ht_lo, 1)

                for j in (3, 4, 5, 6):
                    split_lo(dve, n + j, step)
                hidden(0)
                if extra:
                    extra()
                hidden_lo(0)

                def unit(f, st, tail):
                    for j in (7, 8, 9, 10):
                        split_lo(dve, n + j, st)
                    hidden(f, st)
                    for j in (11, 12)[:2 - tail]:
                        split_lo(dve, n + j, st)
                    hidden_lo(f)

                with dve.Fori(1, UNITS - 1) as f:
                    unit(f, step + f - 1, 0)
                if mid:
                    mid()
                unit(UNITS - 1, step + UNITS - 2, 1 if cut else 0)
                if xtra_end:
                    xtra_end()
                if not cut:
                    split_lo(dve, n + 7, step + UNITS - 1)
                    split_lo(dve, n + 8, step + UNITS - 1)

            def route():
                lg = ps[:, 0, 0:TB * EXPERTS].rearrange("p (b e) -> p b e", b=TB)
                L, idx, first, left = (rt[:, i] for i in range(4))
                oh1, oh2, tmp = (rt[:, i] for i in range(4, 7))
                io = bass.AP(iota.tensor, iota.offset, [iota.ap[0], [0, TB], [1, EXPERTS]])

                def per_token(i):
                    v = r1[:, i, :]
                    return bass.AP(v.tensor, v.offset, [v.ap[0], v.ap[1], [0, EXPERTS]])

                dve.wait_ge(logit_done, 1)
                link(nc.vector.tensor_copy(L, lg))

                def top(src, value, onehot):
                    link(nc.vector.tensor_reduce(r1[:, value, :], src, AX.X, ALU.max))
                    link(nc.vector.tensor_tensor(tmp, src, per_token(value), ALU.is_equal))
                    link(nc.vector.scalar_tensor_tensor(idx, tmp, -float(EXPERTS), io, ALU.mult, ALU.add))
                    link(nc.vector.tensor_reduce(r1[:, 2, :], idx, AX.X, ALU.min))
                    link(nc.vector.tensor_tensor(onehot, idx, per_token(2), ALU.is_equal))

                top(L, 0, oh1)
                link(nc.vector.tensor_scalar(first, oh1, -1.0, 1.0, ALU.mult, ALU.add))
                link(nc.vector.tensor_tensor(left, L, first, ALU.mult))
                link(nc.vector.scalar_tensor_tensor(left, oh1, -3e38, left, ALU.mult, ALU.add))
                top(left, 1, oh2)
                link(nc.vector.tensor_tensor(chosen[:, :, 0:EXPERTS], oh1, oh2, ALU.add))
                nc.vector.memset(chosen[:, :, EXPERTS:EXPERTS + 1], 0.0).then_inc(chosen_done, 1)
                nc.vector.tensor_tensor(r1[:, 4, :], r1[:, 1, :], r1[:, 0, :], ALU.subtract).then_inc(gate_exp_in, 1)
                dve.wait_ge(gate_exp, 1)
                link(nc.vector.tensor_scalar(r1[:, 6, :], r1[:, 5, :], 1.0, None, ALU.add))
                link(nc.vector.reciprocal(r1[:, 7, :], r1[:, 6, :]))
                link(nc.vector.tensor_tensor(r1[:, 3, :], r1[:, 5, :], r1[:, 7, :], ALU.mult))
                link(nc.vector.tensor_tensor(tmp, oh1, per_token(7), ALU.mult))
                link(nc.vector.tensor_tensor(first, oh2, per_token(3), ALU.mult))
                link(nc.vector.tensor_tensor(gates[:, :, 0:EXPERTS], tmp, first, ALU.add))
                dve.wait_ge(pos_done, 1)
                nc.vector.memset(pos[:, :, EXPERTS:EXPERTS + 1], 0.0)
                cnt = ps[:, 1, 0:3 * EXPERTS]
                nc.vector.tensor_copy(pos[:, :, 0:EXPERTS], cnt[:, 0:TB * EXPERTS].rearrange("p (b e) -> p b e", b=TB))
                link(nc.vector.tensor_reduce(full[:, 0:1], cnt[:, 2 * EXPERTS:3 * EXPERTS], AX.X, ALU.max))
                link(nc.vector.tensor_scalar(full_i[:, :], full[:, 0:1], float(PASS_SLOTS), None, ALU.is_gt))
                nc.vector.memset(full[:, 1:2], 0.0).then_inc(routed, 1)

            def make_pick(it, p, e):
                for b in range(TB):
                    src = iota
                    ins = nc.vector.tensor_scalar(pick[:, b, :], src, pos[:, b, bass.ds(e, 1)],
                                                  chosen[:, b, bass.ds(e, 1)], ALU.is_equal, ALU.mult)
                ins.then_inc(pick_done, 1)

            def gathered_lo(it):
                for g in range(2):
                    dve.wait_ge(ga_hi, 2 * it + g + 1)
                    nc.vector.tensor_tensor(xT_lo[:, 4 * g:4 * g + 4, 0:P], bank(1 + 2 * g).rearrange("p (k s) -> p k s", s=P),
                                            xT_hi[:, 4 * g:4 * g + 4, 0:P].bitcast(F32), ALU.subtract).then_inc(ga_lo, 1)

            def accumulate(it, e):
                for b in range(TB):
                    for g in range(2):
                        dve.wait_ge(sct_done, 4 * it + 2 * b + g + 1)
                        if not (isinstance(it, int) and it == 0):
                            dve.wait_ge(x_acc, 4 * it)
                        cols = slice(512 * g, 512 * g + 512)
                        src = bank(6 + g) if b == 0 else bank(1 + 2 * g)
                        nc.vector.scalar_tensor_tensor(x[:, b, cols], src, gates[:, b, bass.ds(e, 1)], x[:, b, cols],
                                                       ALU.mult, ALU.add).then_inc(x_acc, 1)

            def expert_of(p):
                def expert(dve, it, first, last):
                    e = it - p * EXPERTS

                    def previous():
                        if not first:
                            accumulate(it - 1, e - 1)

                    def pick_next():
                        if not last:
                            dve.wait_ge(st_done, it + 1)
                            make_pick(it + 1, p, e + 1)

                    def gather_next():
                        if not last:
                            gathered_lo(it + 1)

                    ffn(MOE, EXPERT_STEPS * it, DENSE_UNITS + UNITS * it, 1, extra=previous, cut=last,
                        xtra_end=gather_next, mid=pick_next)
                return expert

            for n in range(LEAD):
                split_lo(dve, n)
            dve.wait_ge(const_in, 16)
            attention(0)
            norm(1)
            transposed_lo(1)
            ffn(FIRST_TILE["ffn0"], 0, 0, TB)
            add_to_x((FIRST_TILE["attn1"] - 1,) * 2, 4)
            attention(1)
            dve.wait_ge(rw_hi, 1)
            nc.vector.tensor_tensor(wr_lo[:, :, :], wr[:, :, :], wr_hi[:, :, :].bitcast(F32), ALU.subtract).then_inc(rw_lo, 1)
            norm(3)
            transposed_lo(3)
            route()
            dve.wait_ge(routed, 1)
            make_pick(0, 0, 0)
            gathered_lo(0)
            passes(expert_of(0), dve, 0)
            accumulate(EXPERTS - 1, EXPERTS - 1)
            dve.wait_ge(x_acc, 4 * EXPERTS)
            more = dve.value_load(full_i[0:1, 0:1], min_val=0, max_val=1)
            with dve.If(more == 1):
                nc.vector.tensor_scalar(pos[:, :, :], pos[:, :, :], -float(PASS_SLOTS), None, ALU.add).then_inc(dve_step, 1)
                dve.wait_ge(dve_step, chain[0] + 1)
                for n in range(LEAD):
                    split_lo(dve, MOE + n, EXPERT_STEPS * EXPERTS)
                make_pick(EXPERTS, 1, 0)
                gathered_lo(EXPERTS)
                passes(expert_of(1), dve, 1)
                accumulate(2 * EXPERTS - 1, EXPERTS - 1)
                dve.wait_ge(x_acc, 8 * EXPERTS)
            nc.vector.memset(full[:, 1:2], 0.0).then_inc(x_updated, 1)
            norm(4)

        @block.tensor
        def _(pe):
            def tile_ready(n, step=0):
                pe.wait_ge(lo_ready, n + 1 + UNIT_TILES * step)

            def transpose_x(k):
                pe.wait_ge(xn_ready, TB * (k + 1))
                for g in range(4):
                    for c in range(2):
                        for b in range(TB):
                            last = nc.tensor.transpose(ps[:, g, c * SEQ + b * P:c * SEQ + (b + 1) * P],
                                                       xn[:, b, (2 * g + c) * P:(2 * g + c + 1) * P], ident)
                    last.then_inc(tr_done, 1)

            def multiply(n, step, cols, acts, k0, outs, first, last):
                tile_ready(n, step)
                hi, lo = hi_of(n, cols), lo_of(n, cols)
                K = hi.shape[1]
                for b, o in enumerate(outs):
                    for k in range(K):
                        ins = product(o, acts[0][:, k0 + k, tok[b]], acts[1][:, k0 + k, tok[b]], hi[:, k, :], lo[:, k, :],
                                      first and k == 0, last and k == K - 1)
                ins.then_inc(used, 1)

            xT = (xT_hi, xT_lo)
            uT = (uT_hi, uT_lo)

            def attention(layer):
                n = FIRST_TILE[f"attn{layer}"]
                transpose_x(2 * layer)
                pe.wait_ge(tr_lo, 4 * (2 * layer + 1))
                for g in range(N_IN + 1):
                    w = 512 if g < N_IN else REST
                    halves = 2 if g < N_IN else 1
                    if g >= 2:
                        pe.wait_ge(z_out, 10 * layer + 2 * (g - 1))
                    outs = [bank(4 + 2 * (g % 2) + b, w) for b in range(TB)]
                    for half in range(halves):
                        multiply(n, 0, w, xT, 4 * half, outs, half == 0, half == halves - 1)
                        n += 1
                pe.wait_ge(lat_ready, 4 * (layer + 1))
                for g in range(3):
                    for c in range(2 * g, min(2 * g + 2, LC)):
                        for b in range(TB):
                            last = nc.tensor.transpose(ps[:, g, (c % 2) * SEQ + b * P:(c % 2) * SEQ + (b + 1) * P],
                                                       z[:, b, c * P:(c + 1) * P], ident)
                    last.then_inc(lt_done, 1)
                pe.wait_ge(z_out, 10 * (layer + 1))
                pe.wait_ge(lt_lo, 3 * (layer + 1))
                for j in range(2):
                    multiply(n, 0, Q_LORA, uT, 0, [bank(4 + 2 * j + b, Q_LORA) for b in range(TB)], True, True)
                    n += 1
                tile_ready(n)
                hi, lo = hi_of(n, 2 * CA), lo_of(n, 2 * CA)
                for g in range(2):
                    for b in range(TB):
                        for k in range(2):
                            ins = product(bank(2 * g + b), uT_hi[:, QC + k, tok[b]], uT_lo[:, QC + k, tok[b]],
                                          hi[:, k, 512 * g:512 * g + 512], lo[:, k, 512 * g:512 * g + 512], k == 0, k == 1)
                ins.then_inc(used, 1)
                n += 1
                pe.wait_ge(q_roped, 2 * (layer + 1))
                pe.wait_ge(k_roped, 2 * (layer + 1))
                pe.wait_ge(kv_out, 4 * (layer + 1))
                for s in range(HEAD_STEPS + 4):
                    i = HEAD_STEPS * layer + s
                    if s < HEAD_STEPS:
                        ca, h = HEAD_ORDER[s]
                        d = head_dims(ca)
                        if i >= 2:
                            pe.wait_ge(qk_out, i - 1)
                        for b in range(TB):
                            if ca:
                                q, k = z[:, b, CA_Q + h * d:CA_Q + (h + 1) * d], z[:, b, CA_K + h * d:CA_K + (h + 1) * d]
                            else:
                                q, k = q_mla[:, b, h * d:(h + 1) * d], k_mla[:, b, h, :]
                            nc.tensor.transpose(ps[0:d, i % 2, b * P:(b + 1) * P], q, ident)
                            last = nc.tensor.transpose(ps[0:d, i % 2, SEQ + b * P:SEQ + (b + 1) * P], k, ident)
                        last.then_inc(qk_done, 1)
                    if 1 <= s < HEAD_STEPS + 1:
                        j = i - 1
                        d = head_dims(HEAD_ORDER[s - 1][0])
                        pe.wait_ge(qk_out, j + 1)
                        if j >= 2:
                            pe.wait_ge(sc_out, j - 1)
                        qk = qkT[0:d, j % 2, :]
                        nc.tensor.matmul(ps[:, 2 + j % 2, 0:P], qk[:, 0:P], qk[:, SEQ:SEQ + P], start=True, stop=True)
                        nc.tensor.matmul(ps[:, 2 + j % 2, P:SCORES], qk[:, P:SEQ], qk[:, SEQ:2 * SEQ], start=True, stop=True).then_inc(sc_done, 1)
                    if 3 <= s < HEAD_STEPS + 3:
                        j = i - 3
                        pe.wait_ge(p_ready, j + 1)
                        if j >= 2:
                            pe.wait_ge(pT_out, j - 1)
                        for c in range(3):
                            last = nc.tensor.transpose(ps[:, 4 + j % 2, c * P:(c + 1) * P], s_sb[:, j % 3, c * P:(c + 1) * P], ident)
                        last.then_inc(pT_done, 1)
                    if s >= 4:
                        j = i - 4
                        ca, h = HEAD_ORDER[s - 4]
                        pe.wait_ge(pT_out, j + 1)
                        if j >= 2:
                            pe.wait_ge(o_lo, j - 1)
                        pair = slice(P * (h // 2), P * (h // 2) + P)
                        v = z[:, :, CA_V:CA_V + CA] if ca else v_mla[:, :, :]
                        nc.tensor.matmul(ps[:, 6 + j % 2, 0:SEQ], v[:, 0, pair], pT[:, j % 2, 0:SEQ], start=True, stop=False)
                        nc.tensor.matmul(ps[:, 6 + j % 2, P:SEQ], v[:, 1, pair], pT[:, j % 2, SEQ:SCORES], start=False, stop=True).then_inc(o_done, 1)
                pe.wait_ge(o_lo, HEAD_STEPS * (layer + 1))
                for g in range(2):
                    for half in range(2):
                        multiply(n, 0, 512, xT, 4 * half, [bank(2 * g + b) for b in range(TB)], half == 0, half == 1)
                        n += 1

            def ffn(n, step, u0, blocks, extra=None, xtra_end=None, y_wait=None):
                def up(n, st, first_bank, free, f):
                    if not _is_zero(u0, f):
                        pe.wait_ge(free, u0 + blocks * f)
                    for half in range(2):
                        multiply(n + half, st, 512, xT, 4 * half, [bank(first_bank + b) for b in range(blocks)], half == 0, half == 1)

                def transpose_hidden(f):
                    for b in range(blocks):
                        pe.wait_ge(hid_done, u0 + blocks * f + b + 1)
                        for k in range(4):
                            last = nc.tensor.transpose(ps[:, 2 + b, k * P:(k + 1) * P], hid[:, b, k * P:(k + 1) * P], ident)
                        last.then_inc(ht_done, 1)

                def down(n, st, f, first, last):
                    pe.wait_ge(ht_lo, u0 + blocks * (f + 1))
                    for half in range(2):
                        down_tile(n + half, st, half, first and half == 0, last and half == 1)

                def down_tile(n, st, half, first, last):
                    tile_ready(n, st)
                    hi, lo = hi_of(n, D), lo_of(n, D)
                    for b in range(blocks):
                        for k in range(2):
                            for g in range(2):
                                o = bank(4 + 2 * g + b) if blocks == TB else bank(4 + g)
                                ins = product(o, uT_hi[:, 2 * half + k, tok[b]], uT_lo[:, 2 * half + k, tok[b]],
                                              hi[:, k, 512 * g:512 * g + 512], lo[:, k, 512 * g:512 * g + 512],
                                              first and k == 0, last and k == 1)
                    ins.then_inc(used, 1)

                up(n, step, 0, silu_done, 0)
                up(n + 2, step, 2, ht_lo, 0)
                if extra:
                    extra()
                transpose_hidden(0)
                if y_wait:
                    y_wait()

                def unit(f, st, first):
                    up(n + 4, st, 0, silu_done, f)
                    up(n + 6, st, 2, ht_lo, f)
                    down(n + 8, st, f - 1, first, False)
                    transpose_hidden(f)

                unit(1, step, True)
                with pe.Fori(2, UNITS) as f:
                    unit(f, step + f - 1, False)
                if xtra_end:
                    xtra_end()
                down(n + 4, step + UNITS - 1, UNITS - 1, False, True)

            def gather(it):
                pe.wait_ge(pick_done, it + 1)
                for c in range(DC):
                    for b in range(TB):
                        last = nc.tensor.matmul(ps[:, 1 + 2 * (c // 4), (c % 4) * P:(c % 4 + 1) * P], xn[:, b, c * P:(c + 1) * P],
                                                pick[:, b, :], start=(b == 0), stop=(b == TB - 1))
                    if c % 4 == 3:
                        last.then_inc(ga_done, 1)

            def scatter(it):
                pe.wait_ge(y_out, 2 * (it + 1))
                pe.wait_ge(st_out, it + 1)
                for b in range(TB):
                    for g in range(2):
                        o = bank(6 + g) if b == 0 else bank(1 + 2 * g)
                        nc.tensor.matmul(o, pickT[:, b * P:(b + 1) * P], y_sb[:, 512 * g:512 * g + 512],
                                         start=True, stop=True).then_inc(sct_done, 1)

            def expert(pe, it, first, last):
                def between():
                    if not first:
                        scatter(it - 1)
                        pe.wait_ge(x_acc, 4 * it - 3)
                    for b in range(TB):
                        ins = nc.tensor.transpose(ps[:, 6, b * P:(b + 1) * P], pick[:, b, :], ident)
                    ins.then_inc(st_done, 1)

                def gather_next():
                    if not last:
                        if not first:
                            pe.wait_ge(x_acc, 4 * it)
                        gather(it + 1)

                def y_free():
                    if not first:
                        pe.wait_ge(y_out, 2 * it)

                pe.wait_ge(ga_lo, 2 * (it + 1))
                ffn(MOE, EXPERT_STEPS * it, DENSE_UNITS + UNITS * it, 1, extra=between, xtra_end=gather_next, y_wait=y_free)
                if last:
                    scatter(it)

            pe.wait_ge(const_in, 16)
            attention(0)
            transpose_x(1)
            pe.wait_ge(tr_lo, 8)
            ffn(FIRST_TILE["ffn0"], 0, 0, TB)
            attention(1)
            transpose_x(3)
            pe.wait_ge(tr_lo, 16)
            pe.wait_ge(rw_lo, 1)
            for b in range(TB):
                for c in range(DC):
                    for i, (a, w) in enumerate(((xT_hi, wr_hi), (xT_hi, wr_lo), (xT_lo, wr_hi), (xT_lo, wr_lo))):
                        ins = nc.tensor.matmul(ps[:, 0, b * EXPERTS:(b + 1) * EXPERTS], a[:, c, tok[b]], w[:, c, :],
                                               start=(c == 0 and i == 0), stop=(c == DC - 1 and i == 3))
            ins.then_inc(logit_done, 1)
            pe.wait_ge(chosen_done, 1)
            first, second = chosen[:, 0, 0:EXPERTS], chosen[:, 1, 0:EXPERTS]
            nc.tensor.matmul(ps[:, 1, 0:EXPERTS], tri, first, start=True, stop=True)
            nc.tensor.matmul(ps[:, 1, EXPERTS:2 * EXPERTS], ones, first, start=True, stop=False)
            nc.tensor.matmul(ps[:, 1, EXPERTS:2 * EXPERTS], tri, second, start=False, stop=True)
            nc.tensor.matmul(ps[:, 1, 2 * EXPERTS:3 * EXPERTS], ones, first, start=True, stop=False)
            nc.tensor.matmul(ps[:, 1, 2 * EXPERTS:3 * EXPERTS], ones, second, start=False, stop=True).then_inc(pos_done, 1)
            pe.wait_ge(routed, 1)
            gather(0)
            passes(expert, pe, 0)
            more = pe.value_load(full_i[0:1, 0:1], min_val=0, max_val=1)
            with pe.If(more == 1):
                pe.wait_ge(x_acc, 4 * EXPERTS)
                gather(EXPERTS)
                passes(expert, pe, 1)


def _is_zero(u0, f):
    return isinstance(u0, int) and u0 == 0 and isinstance(f, int) and f == 0


def _constants():
    c = np.zeros((P, C_ALL), np.float32)
    c[:, C_ID:C_ID + P] = np.eye(P)
    for diagonal in (0, 2 * P):
        c[0:CHUNK, C_MASK + diagonal + CHUNK:C_MASK + diagonal + P] = NEG
    c[:, C_TRI:C_TRI + P] = np.triu(np.ones((P, P)), 1)
    c[:, C_ONE:C_ONE + P] = 1
    c[:, C_IOTA:C_IOTA + P] = np.arange(P)
    inv = (1.0 / (np.float32(10000.0) ** (np.arange(0, ROPE, 2, dtype=np.float32) / np.float32(ROPE)))).astype(np.float32)
    ang = np.arange(SEQ, dtype=np.float32)[:, None] * inv[None, :]
    for at, f in ((C_COS, np.cos), (C_SIN, np.sin)):
        c[:, at:at + TB * HALF] = f(ang).reshape(TB, P, HALF).transpose(1, 0, 2).reshape(P, TB * HALF)
    return c


_INS = ["x", "attn_norm", "w_in", "q_norm", "w_uq", "kv_norm", "w_ukv", "w_out", "ffn_norm",
        "dense_w1", "dense_w3", "dense_w2", "w_router", "moe_w1", "moe_w3", "moe_w2"]


def kernel(**inputs):
    import concourse.bacc as _bacc
    from concourse.bass_utils import run_bass_kernel_spmd as _run

    nc = _bacc.Bacc("TRN2", target_bir_lowering=False, num_devices=1)
    arrays = {n: np.ascontiguousarray(inputs[n]) for n in _INS}
    arrays["final_norm"] = np.ascontiguousarray(inputs["final_norm"]).reshape(1, D)
    arrays["rel_rev"] = np.ascontiguousarray(np.asarray(inputs["rel_bias"])[:, :, ::-1]).reshape(DEPTH * HEADS, 2 * REL + 1)
    arrays["const"] = _constants()
    t = {n: nc.dram_tensor(f"in_{n}", a.shape, mybir.dt.from_np(a.dtype), kind="ExternalInput").ap() for n, a in arrays.items()}
    out = nc.dram_tensor("out_y", (1, SEQ, D), F32, kind="ExternalOutput").ap()
    build(nc, t, out)
    r = _run(nc, [{f"in_{n}": a for n, a in arrays.items()}], core_ids=[0])
    return r.results[0]["out_y"]
```

```python
from contextlib import ExitStack

import concourse.bass as bass
import numpy as np
from concourse import mybir

F32 = mybir.dt.float32
F32R = mybir.dt.float32r
I32 = mybir.dt.int32
ALU = mybir.AluOpType
ACT = mybir.ActivationFunctionType
AX = mybir.AxisListType

P = 128
D = 1024
SEQ = 256
TB = SEQ // P
DC = D // P
DEPTH = 2
Q_LORA, KV_LORA, ROPE = 384, 256, 32
LATENT = Q_LORA + KV_LORA
LC = LATENT // P
QC = Q_LORA // P
HEADS, HD, NOPE = 8, 64, 64
QK_MLA = NOPE + ROPE
CA = HEADS * HD
IN_DIM = LATENT + ROPE + 3 * CA
CA_Q, CA_K, CA_V = LATENT + ROPE, LATENT + ROPE + CA, LATENT + ROPE + 2 * CA
HALF = ROPE // 2
CHUNK = 64
REL = 128
FFN = 3584
EXPERTS = 8
EPS = 1e-6
NEG = -1e30

TILE = 2048
N_IN = 4
REST = IN_DIM - N_IN * 512
ATTN_TILES = 2 * N_IN + 1 + 2 + 1 + 4
UNIT = 512
UNITS = FFN // UNIT
UNIT_TILES = 6
FFN_TILES = UNIT_TILES * UNITS
RAW, HI, LO = 6, 3, 3
LEAD = 3
HEAD_STEPS = 2 * HEADS
W_OUT_ORDER = [(0, 1), (0, 0), (1, 0), (1, 1)]
SCORES = P + SEQ
NORMS = 5
PERIOD = 3 * P
PASS_SLOTS = P

C_ID, C_MASK, C_TRI, C_ONE, C_IOTA = 0, P, P + SCORES, 2 * P + SCORES, 3 * P + SCORES
C_COS = C_IOTA + P
C_SIN = C_COS + TB * HALF
C_ALL = C_SIN + TB * HALF

FIRST_TILE = {"attn0": 0, "ffn0": ATTN_TILES, "attn1": ATTN_TILES + FFN_TILES,
              "moe": 2 * ATTN_TILES + FFN_TILES}


def build(nc, t, out):
    with ExitStack() as ctx:
        def sb(name, shape, dt=F32):
            return ctx.enter_context(nc.sbuf_tensor(name, shape, dt))

        def sem(name):
            return ctx.enter_context(nc.semaphore(name))

        raw = sb("raw", [P, RAW, TILE])
        w_hi = sb("w_hi", [P, HI, TILE], F32R)
        w_lo = sb("w_lo", [P, LO, TILE], F32R)
        x = sb("x", [P, TB, D])
        xn = sb("xn", [P, TB, D])
        xT_hi = sb("xT_hi", [P, DC, SEQ], F32R)
        xT_lo = sb("xT_lo", [P, DC, SEQ], F32R)
        z = sb("z", [P, TB, IN_DIM])
        uT_hi = sb("uT_hi", [P, LC, SEQ], F32R)
        uT_lo = sb("uT_lo", [P, LC, SEQ], F32R)
        k_mla = sb("k_mla", [P, TB, HEADS, QK_MLA])
        v_mla = sb("v_mla", [P, TB, HEADS * HD])
        bias = sb("bias", [P, HEADS, SCORES])
        const = sb("const", [P, C_ALL])
        gain = sb("gain", [P, D])
        lat_gain = sb("lat_gain", [P, LATENT])
        qkT = sb("qkT", [P, 2, 2 * SEQ])
        s_sb = sb("s_sb", [P, 3, SCORES])
        pT = sb("pT", [P, 2, SCORES])
        rot = sb("rot", [P, 4, P])
        neg_max = sb("neg_max", [P, 3, TB])
        p_sum = sb("p_sum", [P, 3, TB])
        p_inv = sb("p_inv", [P, 3, TB])
        n_ss = sb("n_ss", [P, 2, TB])
        n_sum = sb("n_sum", [P, TB])
        n_ms = sb("n_ms", [P, TB])
        n_sd = sb("n_sd", [P, TB])
        n_inv = sb("n_inv", [P, NORMS, TB])
        l_ss = sb("l_ss", [P, 4])
        l_ms = sb("l_ms", [P, 4])
        l_sd = sb("l_sd", [P, 4])
        l_inv = sb("l_inv", [P, 4])
        ext = sb("ext", [DEPTH * HEADS, PERIOD])
        wr = sb("wr", [P, DC, EXPERTS])
        wr_parts = sb("wr_parts", [P, DC, 2, EXPERTS], F32R)
        rt = sb("rt", [P, 8, TB, EXPERTS])
        r1 = sb("r1", [P, 8, TB])
        chosen = sb("chosen", [P, TB, EXPERTS + 1])
        gates = sb("gates", [P, TB, EXPERTS + 1])
        pos = sb("pos", [P, TB, EXPERTS + 1])
        full = sb("full", [P, 2])
        full_i = sb("full_i", [P, 1], I32)
        ps = ctx.enter_context(nc.psum_tensor("ps", [P, 8, 512], F32))
        ext_dram = nc.dram_tensor("ext_dram", [DEPTH * HEADS, P * PERIOD], F32, kind="Internal").ap()

        ident = const[:, C_ID:C_ID + P]
        mask = const[:, C_MASK:C_MASK + SCORES]
        tri = const[:, C_TRI:C_TRI + P]
        ones = const[:, C_ONE:C_ONE + P]
        iota = const[:, C_IOTA:C_IOTA + P]
        cos = const[:, C_COS:C_SIN].rearrange("p (b j) -> p b j", b=TB)
        sin = const[:, C_SIN:C_ALL].rearrange("p (b j) -> p b j", b=TB)
        q_mla = xn[:, :, 0:HEADS * QK_MLA]
        z_flat = z[:, :, :].rearrange("p b n -> p (b n)")
        silu = z_flat[:, 0:2 * UNIT].rearrange("p (b n) -> p b n", b=TB)
        hid = z_flat[:, 2 * UNIT:4 * UNIT].rearrange("p (b n) -> p b n", b=TB)
        junk = z_flat[:, 0:4 * UNIT].rearrange("p (h b n) -> p h b n", h=2, b=TB)
        y_hi = [a[:, 0:4, P:SEQ] for a in (uT_hi, xT_hi)]
        y_lo = [a[:, 0:4, P:SEQ] for a in (uT_lo, xT_lo)]
        pick = z_flat[:, 6 * UNIT:6 * UNIT + SEQ].rearrange("p (b s) -> p b s", b=TB)
        pickT = uT_hi[:, LC - 1, :]

        landed = [sem(f"landed{i}") for i in range(RAW)]
        hi_ready = sem("hi_ready")
        lo_ready = sem("lo_ready")
        used = sem("used")
        const_in = sem("const_in")
        x_in = [sem(f"x_in{h}") for h in range(2)]
        gain_in = sem("gain_in")
        lat_gain_in = sem("lat_gain_in")
        rel_in = sem("rel_in")
        router_in = sem("router_in")
        ext_done = sem("ext_done")
        ext_out = sem("ext_out")
        bias_in = sem("bias_in")
        bias_ready = sem("bias_ready")
        x_updated = sem("x_updated")
        y_half = sem("y_half")
        xg_ready = sem("xg_ready")
        norm_inv = sem("norm_inv")
        norm_ss = sem("norm_ss")
        norm_ms = sem("norm_ms")
        norm_sd = sem("norm_sd")
        xn_ready = sem("xn_ready")
        xn_out0 = sem("xn_out0")
        xn_out1 = sem("xn_out1")
        lat_ss = sem("lat_ss")
        lat_ms = sem("lat_ms")
        lat_sd = sem("lat_sd")
        lat_ready = sem("lat_ready")
        tr_done = sem("tr_done")
        tr_hi = sem("tr_hi")
        tr_lo = sem("tr_lo")
        z_out = sem("z_out")
        lt_done = sem("lt_done")
        lt_hi = sem("lt_hi")
        lt_lo = sem("lt_lo")
        q_out = sem("q_out")
        kv_out = sem("kv_out")
        k_roped = sem("k_roped")
        q_roped = sem("q_roped")
        qk_done = sem("qk_done")
        qk_out = sem("qk_out")
        sc_done = sem("sc_done")
        sc_out = sem("sc_out")
        max_done = sem("max_done")
        exp_done = sem("exp_done")
        p_ready = sem("p_ready")
        pT_done = sem("pT_done")
        pT_out = sem("pT_out")
        o_done = sem("o_done")
        o_hi = sem("o_hi")
        o_lo = sem("o_lo")
        silu_done = sem("silu_done")
        hid_done = sem("hid_done")
        ht_done = sem("ht_done")
        ht_hi = sem("ht_hi")
        ht_lo = sem("ht_lo")
        rw_hi = sem("rw_hi")
        rw_lo = sem("rw_lo")
        logit_done = sem("logit_done")
        gate_exp_in = sem("gate_exp_in")
        gate_exp = sem("gate_exp")
        chosen_done = sem("chosen_done")
        pos_done = sem("pos_done")
        counted = sem("counted")
        routed = sem("routed")
        pos_moved = sem("pos_moved")
        pick_done = sem("pick_done")
        ga_done = sem("ga_done")
        ga_hi = sem("ga_hi")
        ga_lo = sem("ga_lo")
        st_done = sem("st_done")
        st_out = sem("st_out")
        y_hi_out = sem("y_hi_out")
        y_lo_out = sem("y_lo_out")
        sct_done = sem("sct_done")
        x_acc = sem("x_acc")
        dve_step = sem("dve_step")
        out_stored = sem("out_stored")

        def width(n):
            for base in (FIRST_TILE["attn0"], FIRST_TILE["attn1"]):
                k = n - base
                if 0 <= k < ATTN_TILES:
                    if k == 2 * N_IN:
                        return DC * REST
                    if k in (2 * N_IN + 1, 2 * N_IN + 2):
                        return QC * Q_LORA
            return TILE

        def hi_of(n, cols):
            w = width(n)
            return w_hi[:, n % HI, 0:w].rearrange("p (k n) -> p k n", n=cols)

        def lo_of(n, cols):
            w = width(n)
            return w_lo[:, n % LO, 0:w].rearrange("p (k n) -> p k n", n=cols)

        def load(eng, n, step, src):
            if n >= RAW:
                eng.wait_ge(lo_ready, n - RAW + 1 + UNIT_TILES * step)
            shape = src.shape
            dst = raw[:, n % RAW, 0:width(n)].rearrange("p (k n) -> p k n", n=shape[2])
            eng.dma_start(dst, src).then_inc(landed[n % RAW], 16)

        def round_hi(act, n, step=0):
            act.wait_ge(landed[n % RAW], 16 * (n // RAW + 1) + 16 * (UNIT_TILES // RAW) * step)
            if n >= HI:
                act.wait_ge(used, n - HI + 1 + UNIT_TILES * step)
            w = width(n)
            nc.scalar.activation(w_hi[:, n % HI, 0:w], raw[:, n % RAW, 0:w], ACT.Copy).then_inc(hi_ready, 1)

        def split_lo(dve, n, step=0):
            dve.wait_ge(hi_ready, n + 1 + UNIT_TILES * step)
            if n >= LO:
                dve.wait_ge(used, n - LO + 1 + UNIT_TILES * step)
            w = width(n)
            nc.vector.tensor_tensor(w_lo[:, n % LO, 0:w], raw[:, n % RAW, 0:w],
                                    w_hi[:, n % HI, 0:w].bitcast(F32), ALU.subtract).then_inc(lo_ready, 1)

        def multiplied(eng, n, step=0):
            eng.wait_ge(used, n + 1 + UNIT_TILES * step)

        def product(out_ap, x_hi, x_lo, y_hi, y_lo, start, stop):
            nc.tensor.matmul(out_ap, x_hi, y_hi, start=start, stop=False)
            nc.tensor.matmul(out_ap, x_hi, y_lo, start=False, stop=False)
            return nc.tensor.matmul(out_ap, x_lo, y_hi, start=False, stop=stop)

        def bank(b, n=512):
            return ps[:, b, 0:n]

        half_cols = [slice(0, D // 2), slice(D // 2, D)]
        tok = [slice(b * P, (b + 1) * P) for b in range(TB)]
        HEAD_ORDER = [(True, h) for h in range(HEADS)] + [(False, h) for h in range(HEADS)]

        def head_dims(ca):
            return HD if ca else QK_MLA

        EXPERT_STEPS = UNITS
        MOE = FIRST_TILE["moe"]
        DENSE_UNITS = TB * UNITS

        def passes(emit, eng, p):
            it0 = p * EXPERTS
            emit(eng, it0, True, False)
            with eng.Fori(it0 + 1, it0 + EXPERTS - 1) as it:
                emit(eng, it, False, False)
            emit(eng, it0 + EXPERTS - 1, False, True)

        block = ctx.enter_context(nc.Block())

        @block.sync
        def _(sp):
            x_rows = t["x"].rearrange("a (b p) d -> p (a b) d", p=P)
            for h in range(2):
                sp.dma_start(x[:, :, half_cols[h]], x_rows[:, :, half_cols[h]]).then_inc(x_in[h], 16)
            sp.dma_start(const[:, :], t["const"]).then_inc(const_in, 16)

            def attn_tiles(layer):
                n = FIRST_TILE[f"attn{layer}"]
                w_in = t["w_in"][layer].rearrange("(k p) n -> p k n", p=P)
                for g in range(N_IN):
                    for half in range(2):
                        load(sp, n, 0, w_in[:, 4 * half:4 * half + 4, 512 * g:512 * g + 512])
                        n += 1
                load(sp, n, 0, w_in[:, :, 512 * N_IN:IN_DIM])
                w_uq = t["w_uq"][layer].rearrange("(k p) n -> p k n", p=P)
                for j in range(2):
                    load(sp, n + 1 + j, 0, w_uq[:, :, Q_LORA * j:Q_LORA * (j + 1)])
                load(sp, n + 3, 0, t["w_ukv"][layer].rearrange("(k p) n -> p k n", p=P))
                w_out = t["w_out"][layer].rearrange("(k p) n -> p k n", p=P)
                for i, (g, half) in enumerate(W_OUT_ORDER):
                    load(sp, n + 4 + i, 0, w_out[:, 4 * half:4 * half + 4, 512 * g:512 * g + 512])

            def up_tiles(n, step, w, f):
                w = w.rearrange("(k p) n -> p k n", p=P)
                for half in range(2):
                    load(sp, n + half, step, w[:, 4 * half:4 * half + 4, bass.ds(f * UNIT, UNIT)])

            def down_tiles(n, step, w, f):
                w = w.rearrange("(u k p) n -> u p k n", p=P, k=4)
                for half in range(2):
                    src = w[bass.ds(f, 1), :, 2 * half:2 * half + 2, :]
                    load(sp, n + half, step, src.rearrange("u p k n -> p (u k) n"))

            def ffn_tiles(n, step, w1, w3, w2):
                up_tiles(n, step, w1, 0)
                up_tiles(n + 2, step, w3, 0)
                with sp.Fori(0, UNITS - 1) as f:
                    up_tiles(n + 4, step + f, w1, f + 1)
                    up_tiles(n + 6, step + f, w3, f + 1)
                    down_tiles(n + 8, step + f, w2, f)
                down_tiles(n + 4, step + UNITS - 1, w2, UNITS - 1)

            def expert_tiles(it, e):
                def of(name):
                    return t[name][0, bass.ds(e, 1)].rearrange("e a b -> (e a) b")
                ffn_tiles(MOE, EXPERT_STEPS * it, of("moe_w1"), of("moe_w3"), of("moe_w2"))

            attn_tiles(0)
            ffn_tiles(FIRST_TILE["ffn0"], 0, t["dense_w1"][0], t["dense_w3"][0], t["dense_w2"][0])
            attn_tiles(1)
            with sp.Fori(0, EXPERTS) as e:
                expert_tiles(e, e)
            sp.wait_ge(routed, 1)
            more = sp.value_load(full_i[0:1, 0:1], min_val=0, max_val=1)
            with sp.If(more == 1):
                with sp.Fori(0, EXPERTS) as e:
                    expert_tiles(e + EXPERTS, e)
                sp.wait_ge(x_acc, 2 * 4 * EXPERTS)
            for b in range(TB):
                sp.wait_ge((xn_out0, xn_out1)[b], 1)
                sp.dma_start(out.rearrange("a (b p) d -> p (a b) d", p=P)[:, b, :], xn[:, b, :]).then_inc(out_stored, 16)
            sp.wait_ge(out_stored, 16 * TB)

        @block.gpsimd
        def _(pool):
            def load_gain(k):
                src = [t["attn_norm"][0:1], t["ffn_norm"][0:1], t["attn_norm"][1:2], t["ffn_norm"][1:2], t["final_norm"]][k]
                if k:
                    pool.wait_ge(xg_ready, 4 * k)
                pool.dma_start(gain[:, :], src.to_broadcast([P, D])).then_inc(gain_in, 16)

            def load_lat_gain(layer):
                if layer:
                    pool.wait_ge(lat_ready, 4 * layer)
                pool.dma_start(lat_gain[:, 0:Q_LORA], t["q_norm"][layer:layer + 1].to_broadcast([P, Q_LORA])).then_inc(lat_gain_in, 16)
                pool.dma_start(lat_gain[:, Q_LORA:LATENT], t["kv_norm"][layer:layer + 1].to_broadcast([P, KV_LORA])).then_inc(lat_gain_in, 16)

            def load_bias(layer):
                if layer:
                    pool.wait_ge(sc_out, HEAD_STEPS * layer)
                for first, base, n in ((0, 2 * REL - 1, P), (P, REL - 1, SEQ)):
                    e = ext_dram[layer * HEADS:(layer + 1) * HEADS, base:base + 1]
                    src = bass.AP(e.tensor, e.offset, [[PERIOD - 1, P], [P * PERIOD, HEADS], [1, n]])
                    pool.dma_start(bias[:, :, first:first + n], src).then_inc(bias_in, 16)
                pool.wait_ge(bias_in, 32 * (layer + 1))
                for diagonal in (0, 2 * P):
                    nc.gpsimd.memset(bias[0:CHUNK, :, diagonal + CHUNK:diagonal + P], NEG).then_inc(bias_ready, 1)

            load_gain(0)
            load_lat_gain(0)
            pool.dma_start(ext[:, REL - 1:PERIOD], t["rel_rev"][:, 0:2 * REL + 1]).then_inc(rel_in, 16)
            pool.dma_start(wr[:, :, :], t["w_router"][0].rearrange("(k p) e -> p k e", p=P)).then_inc(router_in, 16)
            pool.wait_ge(rel_in, 16)
            nc.gpsimd.tensor_copy(ext[:, 0:REL - 1], ext[:, REL - 1:REL].to_broadcast([DEPTH * HEADS, REL - 1])).then_inc(ext_done, 1)
            pool.wait_ge(ext_done, 1)
            rows = bass.AP(ext[:, :].tensor, ext[:, :].offset, [ext[:, :].ap[0], [0, P], [1, PERIOD]])
            pool.dma_start(ext_dram.rearrange("h (r d) -> h r d", r=P), rows).then_inc(ext_out, 16)
            pool.wait_ge(ext_out, 16)
            load_bias(0)
            load_gain(1)
            load_gain(2)
            load_lat_gain(1)
            load_bias(1)
            load_gain(3)
            load_gain(4)
            pool.wait_ge(norm_inv, 4)
            pool.wait_ge(tr_done, 16)
            for b in range(TB):
                nc.gpsimd.tensor_scalar(xn[:, b, :], xn[:, b, :], n_inv[:, 3, b:b + 1], None, ALU.mult).then_inc(xn_ready, 1)

        @block.scalar
        def _(act):
            def squares(k, h, acc=0):
                if k == 0:
                    act.wait_ge(x_in[h], 16)
                elif k < NORMS - 1:
                    act.wait_ge(x_updated, 4 * (k - 1) + TB * (h + 1))
                for b in range(TB):
                    if k == NORMS - 1:
                        act.wait_ge(x_acc, acc + TB * h + b + 1)
                    nc.scalar.activation(junk[:, h, b, :], x[:, b, half_cols[h]], ACT.Square,
                                         accum_out=n_ss[:, h, b:b + 1]).then_inc(norm_ss, 1)

            def root(k):
                act.wait_ge(norm_ms, k + 1)
                nc.scalar.activation(n_sd[:, :], n_ms[:, :], ACT.Sqrt).then_inc(norm_sd, 1)

            def transposed_hi(k, h):
                for g in (2 * h, 2 * h + 1):
                    act.wait_ge(tr_done, 4 * k + g + 1)
                    nc.scalar.activation(xT_hi[:, 2 * g:2 * g + 2, :], bank(4 * (k % 2) + g), ACT.Copy).then_inc(tr_hi, 1)

            def attention(layer):
                n0 = FIRST_TILE[f"attn{layer}"]
                k_norm = 2 * layer

                def z_copy(g):
                    if g == 0:
                        act.wait_ge(norm_inv, k_norm + 1)
                    multiplied(act, n0 + min(2 * g + 1, 2 * N_IN))
                    for b in range(TB):
                        w = 512 if g < N_IN else REST
                        nc.scalar.activation(z[:, b, 512 * g:512 * g + w], bank(4 + 2 * (g % 2) + b, w),
                                             ACT.Copy, scale=n_inv[:, k_norm, b:b + 1]).then_inc(z_out, 1)

                def latents_hi():
                    for g in range(3):
                        act.wait_ge(lt_done, 3 * layer + g + 1)
                        m = min(2, LC - 2 * g)
                        nc.scalar.activation(uT_hi[:, 2 * g:2 * g + m, :], bank(g, m * SEQ), ACT.Copy).then_inc(lt_hi, 1)

                n = n0 + LEAD
                for g in range(N_IN + 1):
                    for half in range(2 if g < N_IN else 1):
                        round_hi(act, n)
                        n += 1
                        if (g, half) == (N_IN - 1, 0):
                            latents_hi()
                    z_copy(g)
                    if g == 1:
                        act.wait_ge(z_out, 10 * layer + 4)
                        for b in range(TB):
                            for j, (a, c) in enumerate(((0, Q_LORA), (Q_LORA, LATENT))):
                                nc.scalar.activation(xn[:, b, a:c], z[:, b, a:c], ACT.Square,
                                                     accum_out=l_ss[:, 2 * j + b:2 * j + b + 1]).then_inc(lat_ss, 1)
                    if g == 2:
                        act.wait_ge(lat_ms, layer + 1)
                        nc.scalar.activation(l_sd[:, :], l_ms[:, :], ACT.Sqrt).then_inc(lat_sd, 1)
                for j in range(2):
                    multiplied(act, n0 + 2 * N_IN + 1 + j)
                    for b in range(TB):
                        nc.scalar.activation(q_mla[:, b, Q_LORA * j:Q_LORA * (j + 1)], bank(2 * j + b, Q_LORA),
                                             ACT.Copy).then_inc(q_out, 1)
                    round_hi(act, n)
                    n += 1

                def kv_copy(g):
                    for b in range(TB):
                        kv = bank(4 + 2 * g + b).rearrange("p (h c) -> p h c", c=2 * HD)
                        nc.scalar.activation(k_mla[:, b, 4 * g:4 * g + 4, 0:NOPE], kv[:, :, 0:HD], ACT.Copy)
                        v = v_mla[:, b, :].rearrange("p (h c) -> p h c", c=HD)
                        nc.scalar.activation(v[:, 4 * g:4 * g + 4, :], kv[:, :, HD:2 * HD], ACT.Copy).then_inc(kv_out, 1)

                nc.scalar.activation(l_sd[:, :], l_ms[:, :], ACT.Exp)
                multiplied(act, n0 + 2 * N_IN + 3)
                for s in range(HEAD_STEPS + 4):
                    i = HEAD_STEPS * layer + s
                    if s < HEAD_STEPS:
                        act.wait_ge(qk_done, i + 1)
                        if i >= 2:
                            act.wait_ge(sc_done, i - 1)
                        d = head_dims(HEAD_ORDER[s][0])
                        nc.scalar.activation(qkT[0:d, i % 2, :], ps[0:d, i % 2, :], ACT.Copy).then_inc(qk_out, 1)
                        if s < 2:
                            kv_copy(s)
                    if 2 <= s < HEAD_STEPS + 2:
                        j = i - 2
                        act.wait_ge(max_done, j + 1)
                        for b, (a, c) in enumerate(((0, P), (P, SCORES))):
                            ins = nc.scalar.activation(s_sb[:, j % 3, a:c], s_sb[:, j % 3, a:c], ACT.Exp,
                                                       bias=neg_max[:, j % 3, b:b + 1], accum_out=p_sum[:, j % 3, b:b + 1])
                        ins.then_inc(exp_done, 1)
                    if 3 <= s < HEAD_STEPS + 3:
                        j = i - 3
                        act.wait_ge(pT_done, j + 1)
                        if j >= 2:
                            act.wait_ge(o_done, j - 1)
                        nc.scalar.activation(pT[:, j % 2, :], bank(4 + j % 2, SCORES), ACT.Copy).then_inc(pT_out, 1)
                    if s >= 4:
                        j = i - 4
                        act.wait_ge(o_done, j + 1)
                        ca, h = HEAD_ORDER[s - 4]
                        r = slice(HD * (h % 2), HD * (h % 2) + HD)
                        c = (HEADS * ca + h) // 2
                        nc.scalar.activation(xT_hi[r, c, :], ps[r, 6 + j % 2, 0:SEQ], ACT.Copy).then_inc(o_hi, 1)
                next_norm = k_norm + 1
                for j in range(3):
                    round_hi(act, n + j)
                squares(next_norm, 0)
                round_hi(act, n + 3)
                transposed_hi(next_norm, 0)
                round_hi(act, n + 4)
                squares(next_norm, 1)
                transposed_hi(next_norm, 1)
                root(next_norm)

            def ffn(n, step, u0, blocks, cut=False, mid=None, xtra_end=None, k_norm=None, ending=None):
                def silu_of(f, st=None):
                    multiplied(act, n + 1 if st is None else n + 5, step if st is None else st)
                    for b in range(blocks):
                        act.wait_ge(hid_done, u0 + blocks * f + b + 1 - blocks) if not _is_zero(u0, f) else None
                        scale = 1.0 if k_norm is None else n_inv[:, k_norm, b:b + 1]
                        nc.scalar.activation(silu[:, b, :], bank(b), ACT.Silu, scale=scale).then_inc(silu_done, 1)

                def hidden_hi(f):
                    for b in range(blocks):
                        act.wait_ge(ht_done, u0 + blocks * f + b + 1)
                        nc.scalar.activation(uT_hi[:, 0:4, tok[b]],
                                             bank(2 + b).rearrange("p (k s) -> p k s", s=P), ACT.Copy).then_inc(ht_hi, 1)

                round_hi(act, n + 3, step)
                if k_norm is not None:
                    act.wait_ge(norm_inv, k_norm + 1)
                silu_of(0)
                for j in (4, 5, 6):
                    round_hi(act, n + j, step)
                hidden_hi(0)

                def unit(f, st, last):
                    round_hi(act, n + 7, st)
                    round_hi(act, n + 8, st)
                    silu_of(f, st)
                    for j in (9, 10, 11):
                        round_hi(act, n + j, st)
                    if not last:
                        round_hi(act, n + 12, st)
                    hidden_hi(f)
                    if last and not cut:
                        round_hi(act, n + 12, st)

                with act.Fori(1, UNITS - 1) as f:
                    unit(f, step + f - 1, False)
                if mid:
                    mid()
                unit(UNITS - 1, step + UNITS - 2, True)
                if xtra_end:
                    xtra_end()
                if ending:
                    ending(lambda j: round_hi(act, n + 7 + j, step + UNITS - 1))
                elif not cut:
                    round_hi(act, n + 7, step + UNITS - 1)
                    round_hi(act, n + 8, step + UNITS - 1)

            def gathered_hi(it):
                for g in range(2):
                    act.wait_ge(ga_done, 2 * it + g + 1)
                    nc.scalar.activation(xT_hi[:, 4 * g:4 * g + 4, 0:P], bank(1 + 2 * g).rearrange("p (k s) -> p k s", s=P),
                                         ACT.Copy).then_inc(ga_hi, 1)

            def expert(act, it, first, last):
                def pick_copy():
                    if not first:
                        act.wait_ge(sct_done, 4 * it)
                    act.wait_ge(st_done, it + 1)
                    nc.scalar.activation(pickT, ps[:, 6, 0:SEQ], ACT.Copy).then_inc(st_out, 1)

                def gather_next():
                    if not last:
                        gathered_hi(it + 1)

                ffn(MOE, EXPERT_STEPS * it, DENSE_UNITS + UNITS * it, 1, cut=last, mid=pick_copy, xtra_end=gather_next)
                if last:
                    nc.scalar.activation(n_sd[:, :], n_ms[:, :], ACT.Sqrt)
                act.wait_ge(y_half, it + 2)
                if not first:
                    act.wait_ge(sct_done, 4 * it)
                for g in range(2):
                    if g == 1:
                        multiplied(act, MOE + 5, EXPERT_STEPS * it + UNITS - 1)
                    nc.scalar.activation(y_hi[g], bank(4 + g).rearrange("p (k s) -> p k s", s=P), ACT.Copy).then_inc(y_hi_out, 1)

            def renew(round_next):
                round_next(0)
                squares(2, 0)
                transposed_hi(2, 0)
                round_next(1)
                squares(2, 1)
                transposed_hi(2, 1)
                root(2)

            round_hi(act, 0)
            transposed_hi(0, 0)
            transposed_hi(0, 1)
            round_hi(act, 1)
            squares(0, 0)
            squares(0, 1)
            round_hi(act, 2)
            root(0)
            attention(0)
            ffn(FIRST_TILE["ffn0"], 0, 0, TB, k_norm=1, ending=renew)
            act.wait_ge(router_in, 16)
            nc.scalar.activation(wr_parts[:, :, 0, :], wr[:, :, :], ACT.Copy).then_inc(rw_hi, 1)
            attention(1)
            act.wait_ge(gate_exp_in, 1)
            nc.scalar.activation(r1[:, 5, :], r1[:, 4, :], ACT.Exp).then_inc(gate_exp, 1)
            nc.scalar.activation(n_sd[:, :], n_ms[:, :], ACT.Silu)
            gathered_hi(0)
            passes(expert, act, 0)
            act.wait_ge(routed, 1)
            more = act.value_load(full_i[0:1, 0:1], min_val=0, max_val=1)
            with act.If(more == 1):
                for n in range(LEAD):
                    round_hi(act, MOE + n, EXPERT_STEPS * EXPERTS)
                gathered_hi(EXPERTS)
                passes(expert, act, 1)
                for h in range(2):
                    squares(4, h, 4 * (2 * EXPERTS - 1))
            with act.If(more == 0):
                for h in range(2):
                    squares(4, h, 4 * (EXPERTS - 1))
            root(4)
            act.wait_ge(xg_ready, 4 * NORMS)
            act.wait_ge(norm_inv, 5)
            nc.scalar.activation(xn[:, 1, :], xn[:, 1, :], ACT.Copy, scale=n_inv[:, 4, 1:2]).then_inc(xn_out1, 1)

        @block.vector
        def _(dve):
            chain = [0]

            def link(ins):
                chain[0] += 1
                ins.then_inc(dve_step, 1)
                dve.wait_ge(dve_step, chain[0])

            def inverse_rms(k):
                dve.wait_ge(norm_ss, 2 * TB * (k + 1))
                link(nc.vector.tensor_tensor(n_sum[:, :], n_ss[:, 0, :], n_ss[:, 1, :], ALU.add))
                nc.vector.tensor_scalar(n_ms[:, :], n_sum[:, :], 1.0 / D, EPS, ALU.mult, ALU.add).then_inc(norm_ms, 1)
                dve.wait_ge(norm_sd, k + 1)
                nc.vector.reciprocal(n_inv[:, k, :], n_sd[:, :]).then_inc(norm_inv, 1)

            def add_half(k, h):
                first_bank = 0 if k % 2 else 4
                for b in range(TB):
                    nc.vector.tensor_tensor(x[:, b, half_cols[h]], bank(first_bank + 2 * h + b), x[:, b, half_cols[h]],
                                            ALU.add).then_inc(x_updated, 1)

            def gain_half(k, h):
                dve.wait_ge(gain_in, 16 * (k + 1))
                if k == 0:
                    dve.wait_ge(x_in[h], 16)
                elif k < NORMS - 1:
                    dve.wait_ge(x_updated, 4 * (k - 1) + TB * (h + 1))
                for b in range(TB):
                    nc.vector.tensor_tensor(xn[:, b, half_cols[h]], x[:, b, half_cols[h]], gain[:, half_cols[h]],
                                            ALU.mult).then_inc(xg_ready, 1)

            def transposed_lo(k, h):
                for g in (2 * h, 2 * h + 1):
                    dve.wait_ge(tr_hi, 4 * k + g + 1)
                    nc.vector.tensor_tensor(xT_lo[:, 2 * g:2 * g + 2, :], bank(4 * (k % 2) + g).rearrange("p (k s) -> p k s", s=SEQ),
                                            xT_hi[:, 2 * g:2 * g + 2, :].bitcast(F32), ALU.subtract).then_inc(tr_lo, 1)

            def rotate(v, shape, out1, out2, done):
                v1, v2 = v[..., 0:HALF], v[..., HALF:ROPE]
                m = int(np.prod(shape))
                c, s = cos, sin
                if len(shape) == 3:
                    c = bass.AP(cos.tensor, cos.offset, [cos.ap[0], cos.ap[1], [0, shape[1]], cos.ap[2]])
                    s = bass.AP(sin.tensor, sin.offset, [sin.ap[0], sin.ap[1], [0, shape[1]], sin.ap[2]])
                    parts = [rot[:, i, 0:m].rearrange("p (b h j) -> p b h j", b=shape[0], h=shape[1]) for i in range(4)]
                else:
                    parts = [rot[:, i, 0:m].rearrange("p (b j) -> p b j", b=shape[0]) for i in range(4)]
                for i, (a, w) in enumerate(((v1, c), (v2, s), (v1, s), (v2, c))):
                    ins = nc.vector.tensor_tensor(parts[i], a, w, ALU.mult)
                link(ins)
                nc.vector.tensor_tensor(out1, parts[0], parts[1], ALU.subtract)
                ins = nc.vector.tensor_tensor(out2, parts[2], parts[3], ALU.add)
                if done is not None:
                    ins.then_inc(done, 1)
                else:
                    link(ins)

            def attention(layer):
                n0 = FIRST_TILE[f"attn{layer}"]
                n = n0 + LEAD

                def latents_lo():
                    for g in range(3):
                        dve.wait_ge(lt_hi, 3 * layer + g + 1)
                        m = min(2, LC - 2 * g)
                        nc.vector.tensor_tensor(uT_lo[:, 2 * g:2 * g + m, :], bank(g, m * SEQ).rearrange("p (k s) -> p k s", s=SEQ),
                                                uT_hi[:, 2 * g:2 * g + m, :].bitcast(F32), ALU.subtract).then_inc(lt_lo, 1)

                for g in range(N_IN + 1):
                    for half in range(2 if g < N_IN else 1):
                        split_lo(dve, n)
                        n += 1
                        if (g, half) == (N_IN - 1, 0):
                            latents_lo()
                    if g == 1:
                        dve.wait_ge(lat_ss, 4 * (layer + 1))
                        nc.vector.tensor_scalar(l_ms[:, 0:2], l_ss[:, 0:2], 1.0 / Q_LORA, EPS, ALU.mult, ALU.add)
                        nc.vector.tensor_scalar(l_ms[:, 2:4], l_ss[:, 2:4], 1.0 / KV_LORA, EPS, ALU.mult, ALU.add).then_inc(lat_ms, 1)
                        k_r = z[:, :, LATENT:LATENT + ROPE]
                        rotate(k_r, (TB, HALF), k_r[..., 0:HALF], k_r[..., HALF:ROPE], None)
                        for b in range(TB):
                            nc.vector.tensor_copy(k_mla[:, b, :, NOPE:QK_MLA],
                                                  z[:, b:b + 1, LATENT:LATENT + ROPE].to_broadcast([P, HEADS, ROPE])).then_inc(k_roped, 1)
                    if g == 2:
                        dve.wait_ge(lat_sd, layer + 1)
                        link(nc.vector.reciprocal(l_inv[:, :], l_sd[:, :]))
                        dve.wait_ge(lat_gain_in, 32 * (layer + 1))
                        for b in range(TB):
                            for j, (a, c) in enumerate(((0, Q_LORA), (Q_LORA, LATENT))):
                                nc.vector.scalar_tensor_tensor(z[:, b, a:c], z[:, b, a:c], l_inv[:, 2 * j + b:2 * j + b + 1],
                                                               lat_gain[:, a:c], ALU.mult, ALU.mult).then_inc(lat_ready, 1)
                for j in range(2):
                    split_lo(dve, n)
                    n += 1
                dve.wait_ge(q_out, 4 * layer + 4)
                for b in range(TB):
                    q = q_mla[:, b, :].rearrange("p (h c) -> p h c", c=QK_MLA)[:, :, NOPE:QK_MLA]
                    v1, v2 = q[:, :, 0:HALF], q[:, :, HALF:ROPE]
                    cb = cos[:, b:b + 1, :].to_broadcast([P, HEADS, HALF])
                    sb_ = sin[:, b:b + 1, :].to_broadcast([P, HEADS, HALF])
                    parts = [rot[:, i, :].rearrange("p (h j) -> p h j", h=HEADS) for i in range(4)]
                    for i, (a, w) in enumerate(((v1, cb), (v2, sb_), (v1, sb_), (v2, cb))):
                        ins = nc.vector.tensor_tensor(parts[i], a, w, ALU.mult)
                    link(ins)
                    nc.vector.tensor_tensor(v1, parts[0], parts[1], ALU.subtract)
                    ins = nc.vector.tensor_tensor(v2, parts[2], parts[3], ALU.add)
                    ins.then_inc(q_roped, 1)
                    dve.wait_ge(q_roped, 2 * layer + b + 1)
                dve.wait_ge(bias_ready, 2 * (layer + 1))
                for s in range(1, HEAD_STEPS + 4):
                    i = HEAD_STEPS * layer + s
                    if s < HEAD_STEPS + 1:
                        j = i - 1
                        ca, h = HEAD_ORDER[s - 1]
                        dve.wait_ge(sc_done, j + 1)
                        if j >= 3:
                            dve.wait_ge(pT_done, j - 2)
                        nc.vector.scalar_tensor_tensor(s_sb[:, j % 3, :], bank(2 + j % 2, SCORES), head_dims(ca) ** -0.5,
                                                       bias[:, h, :] if ca else mask, ALU.mult, ALU.add).then_inc(sc_out, 1)
                        dve.wait_ge(sc_out, j + 1)
                        for b, (a, c) in enumerate(((0, P), (P, SCORES))):
                            ins = nc.vector.tensor_reduce(neg_max[:, j % 3, b:b + 1], s_sb[:, j % 3, a:c], AX.X, ALU.max, negate=True)
                        ins.then_inc(max_done, 1)
                    if 2 <= s < HEAD_STEPS + 2:
                        j = i - 2
                        dve.wait_ge(exp_done, j + 1)
                        link(nc.vector.reciprocal(p_inv[:, j % 3, :], p_sum[:, j % 3, :]))
                        for b, (a, c) in enumerate(((0, P), (P, SCORES))):
                            ins = nc.vector.tensor_scalar(s_sb[:, j % 3, a:c], s_sb[:, j % 3, a:c], p_inv[:, j % 3, b:b + 1], None, ALU.mult)
                        ins.then_inc(p_ready, 1)
                    if s >= 4:
                        j = i - 4
                        dve.wait_ge(o_hi, j + 1)
                        ca, h = HEAD_ORDER[s - 4]
                        r = slice(HD * (h % 2), HD * (h % 2) + HD)
                        c = (HEADS * ca + h) // 2
                        nc.vector.tensor_tensor(xT_lo[r, c, :], ps[r, 6 + j % 2, 0:SEQ], xT_hi[r, c, :].bitcast(F32),
                                                ALU.subtract).then_inc(o_lo, 1)
                k_norm = 2 * layer + 1
                split_lo(dve, n)
                split_lo(dve, n + 1)
                multiplied(dve, n - 1)
                add_half(k_norm, 0)
                gain_half(k_norm, 0)
                split_lo(dve, n + 2)
                split_lo(dve, n + 3)
                transposed_lo(k_norm, 0)
                multiplied(dve, n + 1)
                add_half(k_norm, 1)
                gain_half(k_norm, 1)
                transposed_lo(k_norm, 1)
                split_lo(dve, n + 4)
                inverse_rms(k_norm)

            def ffn(n, step, u0, blocks, extra=None, cut=False, xtra_end=None, mid=None, k_norm=None, ending=None):
                def hidden(f, st=None):
                    multiplied(dve, n + 3 if st is None else n + 7, step if st is None else st)
                    for b in range(blocks):
                        dve.wait_ge(silu_done, u0 + blocks * f + b + 1)
                        if not _is_zero(u0, f):
                            dve.wait_ge(ht_done, u0 + blocks * f + b + 1 - blocks)
                        if k_norm is None:
                            ins = nc.vector.tensor_tensor(hid[:, b, :], bank(2 + b), silu[:, b, :], ALU.mult)
                        else:
                            ins = nc.vector.scalar_tensor_tensor(hid[:, b, :], bank(2 + b), n_inv[:, k_norm, b:b + 1],
                                                                 silu[:, b, :], ALU.mult, ALU.mult)
                        ins.then_inc(hid_done, 1)

                def hidden_lo(f):
                    for b in range(blocks):
                        dve.wait_ge(ht_hi, u0 + blocks * f + b + 1)
                        nc.vector.tensor_tensor(uT_lo[:, 0:4, tok[b]], bank(2 + b).rearrange("p (k s) -> p k s", s=P),
                                                uT_hi[:, 0:4, tok[b]].bitcast(F32), ALU.subtract).then_inc(ht_lo, 1)

                for j in (3, 4, 5):
                    split_lo(dve, n + j, step)
                hidden(0)
                split_lo(dve, n + 6, step)
                hidden_lo(0)
                if extra:
                    extra()

                def unit(f, st, last):
                    for j in (7, 8, 9, 10):
                        split_lo(dve, n + j, st)
                    hidden(f, st)
                    split_lo(dve, n + 11, st)
                    if not last:
                        split_lo(dve, n + 12, st)
                    hidden_lo(f)
                    if last and not cut:
                        split_lo(dve, n + 12, st)

                with dve.Fori(1, UNITS - 1) as f:
                    unit(f, step + f - 1, False)
                if mid:
                    mid()
                unit(UNITS - 1, step + UNITS - 2, True)
                if xtra_end:
                    xtra_end()
                if ending:
                    ending(lambda j: split_lo(dve, n + 7 + j, step + UNITS - 1))
                elif not cut:
                    split_lo(dve, n + 7, step + UNITS - 1)
                    split_lo(dve, n + 8, step + UNITS - 1)

            def make_pick(it, p, e):
                for b in range(TB):
                    ins = nc.vector.tensor_scalar(pick[:, b, :], iota, pos[:, b, bass.ds(e, 1)],
                                                  chosen[:, b, bass.ds(e, 1)], ALU.is_equal, ALU.mult)
                ins.then_inc(pick_done, 1)

            def route():
                L, idx, first, left = (rt[:, i] for i in range(4))
                oh1, oh2, tmp = (rt[:, i] for i in range(4, 7))
                io = bass.AP(iota.tensor, iota.offset, [iota.ap[0], [0, TB], [1, EXPERTS]])

                def per_token(i):
                    v = r1[:, i, :]
                    return bass.AP(v.tensor, v.offset, [v.ap[0], v.ap[1], [0, EXPERTS]])

                dve.wait_ge(logit_done, 1)
                for b in range(TB):
                    ins = nc.vector.tensor_scalar(tmp[:, b, :], ps[:, b, EXPERTS:2 * EXPERTS], n_inv[:, 3, b:b + 1], None, ALU.mult)
                link(ins)
                for b in range(TB):
                    ins = nc.vector.scalar_tensor_tensor(L[:, b, :], ps[:, b, 0:EXPERTS], n_inv[:, 3, b:b + 1], tmp[:, b, :],
                                                         ALU.mult, ALU.add)
                link(ins)

                def top(src, value, onehot):
                    link(nc.vector.tensor_reduce(r1[:, value, :], src, AX.X, ALU.max))
                    link(nc.vector.tensor_tensor(tmp, src, per_token(value), ALU.is_equal))
                    link(nc.vector.scalar_tensor_tensor(idx, tmp, -float(EXPERTS), io, ALU.mult, ALU.add))
                    link(nc.vector.tensor_reduce(r1[:, 2, :], idx, AX.X, ALU.min))
                    link(nc.vector.tensor_tensor(onehot, idx, per_token(2), ALU.is_equal))

                top(L, 0, oh1)
                link(nc.vector.scalar_tensor_tensor(left, oh1, -3e38, L, ALU.mult, ALU.add))
                top(left, 1, oh2)
                link(nc.vector.tensor_tensor(chosen[:, :, 0:EXPERTS], oh1, oh2, ALU.add))
                nc.vector.memset(chosen[:, :, EXPERTS:EXPERTS + 1], 0.0).then_inc(chosen_done, 1)
                nc.vector.tensor_tensor(r1[:, 4, :], r1[:, 1, :], r1[:, 0, :], ALU.subtract).then_inc(gate_exp_in, 1)
                dve.wait_ge(gate_exp, 1)
                link(nc.vector.tensor_scalar(r1[:, 6, :], r1[:, 5, :], 1.0, None, ALU.add))
                link(nc.vector.reciprocal(r1[:, 7, :], r1[:, 6, :]))
                link(nc.vector.tensor_tensor(r1[:, 3, :], r1[:, 5, :], r1[:, 7, :], ALU.mult))
                link(nc.vector.tensor_tensor(tmp, oh1, per_token(7), ALU.mult))
                link(nc.vector.tensor_tensor(first, oh2, per_token(3), ALU.mult))
                link(nc.vector.tensor_tensor(gates[:, :, 0:EXPERTS], tmp, first, ALU.add))
                dve.wait_ge(pos_done, 1)
                nc.vector.memset(pos[:, :, EXPERTS:EXPERTS + 1], 0.0)
                cnt = ps[:, 2, 0:TB * EXPERTS]
                link(nc.vector.tensor_copy(pos[:, :, 0:EXPERTS], cnt.rearrange("p (b e) -> p b e", b=TB)))
                make_pick(0, 0, 0)
                dve.wait_ge(counted, 1)
                link(nc.vector.tensor_reduce(full[:, 0:1], ps[:, 6, 0:EXPERTS], AX.X, ALU.max))
                link(nc.vector.tensor_scalar(full_i[:, :], full[:, 0:1], float(PASS_SLOTS), None, ALU.is_gt))
                nc.vector.memset(full[:, 1:2], 0.0).then_inc(routed, 1)

            def gathered_lo(it):
                for g in range(2):
                    dve.wait_ge(ga_hi, 2 * it + g + 1)
                    nc.vector.tensor_tensor(xT_lo[:, 4 * g:4 * g + 4, 0:P], bank(1 + 2 * g).rearrange("p (k s) -> p k s", s=P),
                                            xT_hi[:, 4 * g:4 * g + 4, 0:P].bitcast(F32), ALU.subtract).then_inc(ga_lo, 1)

            def accumulate(it, e):
                for g in range(2):
                    for b in range(TB):
                        dve.wait_ge(sct_done, 4 * it + 2 * g + b + 1)
                        if not (isinstance(it, int) and it == 0):
                            dve.wait_ge(x_acc, 4 * it)
                        cols = slice(512 * g, 512 * g + 512)
                        src = bank(6 + g) if b == 0 else bank(1 + 2 * g)
                        nc.vector.scalar_tensor_tensor(x[:, b, cols], src, gates[:, b, bass.ds(e, 1)], x[:, b, cols],
                                                       ALU.mult, ALU.add).then_inc(x_acc, 1)

            def expert_of(p):
                def expert(dve, it, first, last):
                    e = it - p * EXPERTS

                    def previous():
                        if not first:
                            accumulate(it - 1, e - 1)

                    def pick_next():
                        if not last:
                            dve.wait_ge(st_done, it + 1)
                            make_pick(it + 1, p, e + 1)

                    def gather_next():
                        if not last:
                            gathered_lo(it + 1)

                    ffn(MOE, EXPERT_STEPS * it, DENSE_UNITS + UNITS * it, 1, extra=previous, cut=last,
                        xtra_end=gather_next, mid=pick_next)
                    for g in range(2):
                        dve.wait_ge(y_hi_out, 2 * it + g + 1)
                        if g == 0 and not first:
                            dve.wait_ge(sct_done, 4 * it)
                        nc.vector.tensor_tensor(y_lo[g], bank(4 + g).rearrange("p (k s) -> p k s", s=P), y_hi[g].bitcast(F32),
                                                ALU.subtract).then_inc(y_lo_out, 1)
                return expert

            def renew(split_next):
                split_next(0)
                dve.wait_ge(y_half, 1)
                add_half(2, 0)
                gain_half(2, 0)
                multiplied(dve, FIRST_TILE["attn1"] - 1)
                add_half(2, 1)
                transposed_lo(2, 0)
                gain_half(2, 1)
                split_next(1)
                transposed_lo(2, 1)
                inverse_rms(2)

            gain_half(0, 0)
            gain_half(0, 1)
            transposed_lo(0, 0)
            split_lo(dve, 0)
            transposed_lo(0, 1)
            split_lo(dve, 1)
            split_lo(dve, 2)
            inverse_rms(0)
            dve.wait_ge(const_in, 16)
            attention(0)
            dve.wait_ge(norm_inv, 2)
            ffn(FIRST_TILE["ffn0"], 0, 0, TB, k_norm=1, ending=renew)
            dve.wait_ge(rw_hi, 1)
            nc.vector.tensor_tensor(wr_parts[:, :, 1, :], wr[:, :, :], wr_parts[:, :, 0, :].bitcast(F32), ALU.subtract).then_inc(rw_lo, 1)
            attention(1)
            dve.wait_ge(norm_inv, 4)
            route()
            dve.wait_ge(routed, 1)
            gathered_lo(0)
            passes(expert_of(0), dve, 0)
            accumulate(EXPERTS - 1, EXPERTS - 1)
            dve.wait_ge(x_acc, 4 * EXPERTS)
            more = dve.value_load(full_i[0:1, 0:1], min_val=0, max_val=1)
            with dve.If(more == 1):
                nc.vector.tensor_scalar(pos[:, :, :], pos[:, :, :], -float(PASS_SLOTS), None, ALU.add).then_inc(pos_moved, 1)
                dve.wait_ge(pos_moved, 1)
                for n in range(LEAD):
                    split_lo(dve, MOE + n, EXPERT_STEPS * EXPERTS)
                make_pick(EXPERTS, 1, 0)
                gathered_lo(EXPERTS)
                passes(expert_of(1), dve, 1)
                accumulate(2 * EXPERTS - 1, EXPERTS - 1)
                dve.wait_ge(x_acc, 8 * EXPERTS)
            gain_half(4, 0)
            gain_half(4, 1)
            inverse_rms(4)
            dve.wait_ge(norm_inv, 5)
            dve.wait_ge(xg_ready, 4 * NORMS)
            nc.vector.tensor_scalar(xn[:, 0, :], xn[:, 0, :], n_inv[:, 4, 0:1], None, ALU.mult).then_inc(xn_out0, 1)

        @block.tensor
        def _(pe):
            def tile_ready(n, step=0):
                pe.wait_ge(lo_ready, n + 1 + UNIT_TILES * step)

            def transpose_x(k, h):
                pe.wait_ge(xg_ready, 4 * k + TB * (h + 1))
                for g in (2 * h, 2 * h + 1):
                    for c in range(2):
                        for b in range(TB):
                            last = nc.tensor.transpose(ps[:, 4 * (k % 2) + g, c * SEQ + b * P:c * SEQ + (b + 1) * P],
                                                       xn[:, b, (2 * g + c) * P:(2 * g + c + 1) * P], ident)
                    last.then_inc(tr_done, 1)

            def multiply(n, step, cols, acts, k0, outs, first, last, between=None):
                tile_ready(n, step)
                hi, lo = hi_of(n, cols), lo_of(n, cols)
                K = hi.shape[1]
                for b, o in enumerate(outs):
                    if b == 1 and between:
                        between()
                    for k in range(K):
                        ins = product(o, acts[0][:, k0 + k, tok[b]], acts[1][:, k0 + k, tok[b]], hi[:, k, :], lo[:, k, :],
                                      first and k == 0, last and k == K - 1)
                ins.then_inc(used, 1)

            xT = (xT_hi, xT_lo)
            uT = (uT_hi, uT_lo)

            def attention(layer):
                n = FIRST_TILE[f"attn{layer}"]
                k_norm = 2 * layer

                def transpose_latents():
                    pe.wait_ge(lat_ready, 4 * (layer + 1))
                    for g in range(3):
                        for c in range(2 * g, min(2 * g + 2, LC)):
                            for b in range(TB):
                                last = nc.tensor.transpose(ps[:, g, (c % 2) * SEQ + b * P:(c % 2) * SEQ + (b + 1) * P],
                                                           z[:, b, c * P:(c + 1) * P], ident)
                        last.then_inc(lt_done, 1)

                for g in range(N_IN + 1):
                    w = 512 if g < N_IN else REST
                    halves = 2 if g < N_IN else 1
                    if g >= 2:
                        pe.wait_ge(z_out, 10 * layer + 2 * (g - 1))
                    outs = [bank(4 + 2 * (g % 2) + b, w) for b in range(TB)]
                    for half in range(halves):
                        if g == 0:
                            pe.wait_ge(tr_lo, 4 * k_norm + 2 * (half + 1))
                        early = g == 0 and half == 0 and k_norm
                        multiply(n, 0, w, xT, 4 * half, outs, half == 0, half == halves - 1,
                                 between=(lambda: transpose_x(k_norm, 1)) if early else None)
                        n += 1
                        if (g, half) == (N_IN - 1, 0):
                            transpose_latents()
                pe.wait_ge(lt_lo, 3 * (layer + 1))
                for j in range(2):
                    multiply(n, 0, Q_LORA, uT, 0, [bank(2 * j + b, Q_LORA) for b in range(TB)], True, True)
                    n += 1
                pe.wait_ge(z_out, 10 * (layer + 1))
                tile_ready(n)
                hi, lo = hi_of(n, 2 * CA), lo_of(n, 2 * CA)
                for g in range(2):
                    for b in range(TB):
                        for k in range(2):
                            ins = product(bank(4 + 2 * g + b), uT_hi[:, QC + k, tok[b]], uT_lo[:, QC + k, tok[b]],
                                          hi[:, k, 512 * g:512 * g + 512], lo[:, k, 512 * g:512 * g + 512], k == 0, k == 1)
                ins.then_inc(used, 1)
                n += 1
                for s in range(HEAD_STEPS + 4):
                    i = HEAD_STEPS * layer + s
                    if s < HEAD_STEPS:
                        ca, h = HEAD_ORDER[s]
                        d = head_dims(ca)
                        if s == HEADS:
                            pe.wait_ge(q_roped, 2 * (layer + 1))
                            pe.wait_ge(k_roped, 2 * (layer + 1))
                            pe.wait_ge(kv_out, 4 * (layer + 1))
                        if s == 0:
                            pe.wait_ge(q_out, 4 * (layer + 1))
                        if i >= 2:
                            pe.wait_ge(qk_out, i - 1)
                        for b in range(TB):
                            if ca:
                                q, k = z[:, b, CA_Q + h * d:CA_Q + (h + 1) * d], z[:, b, CA_K + h * d:CA_K + (h + 1) * d]
                            else:
                                q, k = q_mla[:, b, h * d:(h + 1) * d], k_mla[:, b, h, :]
                            nc.tensor.transpose(ps[0:d, i % 2, b * P:(b + 1) * P], q, ident)
                            last = nc.tensor.transpose(ps[0:d, i % 2, SEQ + b * P:SEQ + (b + 1) * P], k, ident)
                        last.then_inc(qk_done, 1)
                    if 1 <= s < HEAD_STEPS + 1:
                        j = i - 1
                        d = head_dims(HEAD_ORDER[s - 1][0])
                        pe.wait_ge(qk_out, j + 1)
                        if j >= 2:
                            pe.wait_ge(sc_out, j - 1)
                        qk = qkT[0:d, j % 2, :]
                        nc.tensor.matmul(ps[:, 2 + j % 2, 0:P], qk[:, 0:P], qk[:, SEQ:SEQ + P], start=True, stop=True)
                        nc.tensor.matmul(ps[:, 2 + j % 2, P:SCORES], qk[:, P:SEQ], qk[:, SEQ:2 * SEQ], start=True, stop=True).then_inc(sc_done, 1)
                    if 3 <= s < HEAD_STEPS + 3:
                        j = i - 3
                        pe.wait_ge(p_ready, j + 1)
                        if s == 3:
                            pe.wait_ge(kv_out, 4 * (layer + 1))
                        if j >= 2:
                            pe.wait_ge(pT_out, j - 1)
                        for c in range(3):
                            last = nc.tensor.transpose(ps[:, 4 + j % 2, c * P:(c + 1) * P], s_sb[:, j % 3, c * P:(c + 1) * P], ident)
                        last.then_inc(pT_done, 1)
                    if s >= 4:
                        j = i - 4
                        ca, h = HEAD_ORDER[s - 4]
                        pe.wait_ge(pT_out, j + 1)
                        if j >= 2:
                            pe.wait_ge(o_lo, j - 1)
                        pair = slice(P * (h // 2), P * (h // 2) + P)
                        v = z[:, :, CA_V:CA_V + CA] if ca else v_mla[:, :, :]
                        nc.tensor.matmul(ps[:, 6 + j % 2, 0:SEQ], v[:, 0, pair], pT[:, j % 2, 0:SEQ], start=True, stop=False)
                        nc.tensor.matmul(ps[:, 6 + j % 2, P:SEQ], v[:, 1, pair], pT[:, j % 2, SEQ:SCORES], start=False, stop=True).then_inc(o_done, 1)
                    if s >= HEAD_STEPS:
                        if s == HEAD_STEPS:
                            tile_ready(n)
                            pe.wait_ge(o_lo, HEAD_STEPS * layer + HEADS)
                            pe.wait_ge(qk_out, HEAD_STEPS * (layer + 1))
                        hi, lo = hi_of(n, 512), lo_of(n, 512)
                        part = s - HEAD_STEPS
                        for b in range(TB):
                            ins = product(bank(b), xT_hi[:, 4 + part, tok[b]], xT_lo[:, 4 + part, tok[b]],
                                          hi[:, part, :], lo[:, part, :], part == 0, False)
                        if part == 3:
                            ins.then_inc(used, 1)
                n += 1
                pe.wait_ge(o_lo, HEAD_STEPS * (layer + 1))
                for g, half in W_OUT_ORDER[1:]:
                    first = half == W_OUT_ORDER[2 * g][1]
                    multiply(n, 0, 512, xT, 4 * half, [bank(2 * g + b) for b in range(TB)], first, not first)
                    n += 1
                    if (g, half) == (1, 0):
                        transpose_x(k_norm + 1, 0)

            def ffn(n, step, u0, blocks, extra=None, mid=None, xtra_end=None, y_wait=None, k_norm=None, gathered=None):
                def up(n, st, first_bank, free, f):
                    if not _is_zero(u0, f):
                        pe.wait_ge(free, u0 + blocks * f)
                    start = k_norm is not None and isinstance(f, int) and f == 0 and first_bank == 0
                    for half in range(2):
                        if start:
                            pe.wait_ge(tr_lo, 4 * k_norm + 2 * (half + 1))
                        if gathered is not None and isinstance(f, int) and f == 0 and first_bank == 0:
                            pe.wait_ge(ga_lo, 2 * gathered + half + 1)
                        multiply(n + half, st, 512, xT, 4 * half, [bank(first_bank + b) for b in range(blocks)], half == 0, half == 1,
                                 between=(lambda: transpose_x(k_norm, 1)) if start and half == 0 else None)

                def transpose_hidden(f):
                    for b in range(blocks):
                        pe.wait_ge(hid_done, u0 + blocks * f + b + 1)
                        for k in range(4):
                            last = nc.tensor.transpose(ps[:, 2 + b, k * P:(k + 1) * P], hid[:, b, k * P:(k + 1) * P], ident)
                        last.then_inc(ht_done, 1)

                def down(n, st, f, first, last):
                    pe.wait_ge(ht_lo, u0 + blocks * (f + 1))
                    for half in range(2):
                        down_tile(n + half, st, half, first and half == 0, last and half == 1)

                def down_tile(n, st, half, first, last):
                    tile_ready(n, st)
                    hi, lo = hi_of(n, D), lo_of(n, D)
                    order = [(b, k, g) for b in range(blocks) for k in range(2) for g in range(2)]
                    by_half = last
                    if by_half:
                        order = [(b, k, g) for g in range(2) for b in range(blocks) for k in range(2)]
                    for b, k, g in order:
                        o = bank(4 + 2 * g + b) if blocks == TB else bank(4 + g)
                        ins = product(o, uT_hi[:, 2 * half + k, tok[b]], uT_lo[:, 2 * half + k, tok[b]],
                                      hi[:, k, 512 * g:512 * g + 512], lo[:, k, 512 * g:512 * g + 512],
                                      first and k == 0, last and k == 1)
                        if by_half and (g, b, k) == (0, blocks - 1, 1):
                            ins.then_inc(y_half, 1)
                    ins.then_inc(used, 1)

                up(n, step, 0, silu_done, 0)
                up(n + 2, step, 2, ht_lo, 0)
                if extra:
                    extra()
                transpose_hidden(0)
                if y_wait:
                    y_wait()

                def unit(f, st, first):
                    up(n + 4, st, 0, silu_done, f)
                    up(n + 6, st, 2, ht_lo, f)
                    down(n + 8, st, f - 1, first, False)
                    transpose_hidden(f)

                unit(1, step, True)
                if mid:
                    mid()
                with pe.Fori(2, UNITS) as f:
                    unit(f, step + f - 1, False)
                if xtra_end:
                    xtra_end()
                down(n + 4, step + UNITS - 1, UNITS - 1, False, True)

            def gather(it):
                pe.wait_ge(xn_ready, TB)
                pe.wait_ge(pick_done, it + 1)
                for c in range(DC):
                    for b in range(TB):
                        last = nc.tensor.matmul(ps[:, 1 + 2 * (c // 4), (c % 4) * P:(c % 4 + 1) * P], xn[:, b, c * P:(c + 1) * P],
                                                pick[:, b, :], start=(b == 0), stop=(b == TB - 1))
                    if c % 4 == 3:
                        last.then_inc(ga_done, 1)

            def scatter(it):
                pe.wait_ge(st_out, it + 1)
                for g in range(2):
                    pe.wait_ge(y_lo_out, 2 * it + g + 1)
                    for b in range(TB):
                        o = (bank(6 + g) if b == 0 else bank(1 + 2 * g)).rearrange("p (k s) -> p k s", s=P)
                        nc.tensor.matmul(o, pickT[:, b * P:(b + 1) * P], y_hi[g], start=True, stop=False)
                        nc.tensor.matmul(o, pickT[:, b * P:(b + 1) * P], y_lo[g], start=False, stop=True).then_inc(sct_done, 1)

            def expert(pe, it, first, last):
                def scatter_last():
                    if not first:
                        scatter(it - 1)

                def transpose_pick():
                    if not first:
                        pe.wait_ge(x_acc, 4 * it)
                    for b in range(TB):
                        ins = nc.tensor.transpose(ps[:, 6, b * P:(b + 1) * P], pick[:, b, :], ident)
                    ins.then_inc(st_done, 1)

                def gather_next():
                    if not last:
                        if not first:
                            pe.wait_ge(x_acc, 4 * it)
                        gather(it + 1)

                def y_free():
                    if not first:
                        pe.wait_ge(y_lo_out, 2 * it)

                ffn(MOE, EXPERT_STEPS * it, DENSE_UNITS + UNITS * it, 1, extra=scatter_last, mid=transpose_pick, xtra_end=gather_next, y_wait=y_free, gathered=it)
                if last:
                    scatter(it)

            pe.wait_ge(const_in, 16)
            transpose_x(0, 0)
            transpose_x(0, 1)
            attention(0)
            ffn(FIRST_TILE["ffn0"], 0, 0, TB, k_norm=1)
            transpose_x(2, 0)
            attention(1)
            def logits(h):
                for c in range(4 * h, 4 * h + 4):
                    pe.wait_ge(tr_lo, 12 + c // 2 + 1)
                    for b in range(TB):
                        for i, a in enumerate((xT_hi, xT_lo)):
                            ins = nc.tensor.matmul(bank(b, 2 * EXPERTS), a[:, c, tok[b]], wr_parts[:, c, :, :].rearrange("p i e -> p (i e)"),
                                                   start=(c == 0 and i == 0), stop=(c == DC - 1 and i == 1))
                return ins

            pe.wait_ge(rw_lo, 1)
            logits(0)
            transpose_x(3, 1)
            logits(1).then_inc(logit_done, 1)
            pe.wait_ge(chosen_done, 1)
            first, second = chosen[:, 0, 0:EXPERTS], chosen[:, 1, 0:EXPERTS]
            nc.tensor.matmul(ps[:, 2, 0:EXPERTS], tri, first, start=True, stop=True)
            nc.tensor.matmul(ps[:, 2, EXPERTS:2 * EXPERTS], ones, first, start=True, stop=False)
            nc.tensor.matmul(ps[:, 2, EXPERTS:2 * EXPERTS], tri, second, start=False, stop=True).then_inc(pos_done, 1)
            nc.tensor.matmul(ps[:, 6, 0:EXPERTS], ones, first, start=True, stop=False)
            nc.tensor.matmul(ps[:, 6, 0:EXPERTS], ones, second, start=False, stop=True).then_inc(counted, 1)
            gather(0)
            passes(expert, pe, 0)
            pe.wait_ge(routed, 1)
            more = pe.value_load(full_i[0:1, 0:1], min_val=0, max_val=1)
            with pe.If(more == 1):
                pe.wait_ge(x_acc, 4 * EXPERTS)
                gather(EXPERTS)
                passes(expert, pe, 1)


def _is_zero(u0, f):
    return isinstance(u0, int) and u0 == 0 and isinstance(f, int) and f == 0


def _constants():
    c = np.zeros((P, C_ALL), np.float32)
    c[:, C_ID:C_ID + P] = np.eye(P)
    for diagonal in (0, 2 * P):
        c[0:CHUNK, C_MASK + diagonal + CHUNK:C_MASK + diagonal + P] = NEG
    c[:, C_TRI:C_TRI + P] = np.triu(np.ones((P, P)), 1)
    c[:, C_ONE:C_ONE + P] = 1
    c[:, C_IOTA:C_IOTA + P] = np.arange(P)
    inv = (1.0 / (np.float32(10000.0) ** (np.arange(0, ROPE, 2, dtype=np.float32) / np.float32(ROPE)))).astype(np.float32)
    ang = np.arange(SEQ, dtype=np.float32)[:, None] * inv[None, :]
    for at, f in ((C_COS, np.cos), (C_SIN, np.sin)):
        c[:, at:at + TB * HALF] = f(ang).reshape(TB, P, HALF).transpose(1, 0, 2).reshape(P, TB * HALF)
    return c


_INS = ["x", "attn_norm", "w_in", "q_norm", "w_uq", "kv_norm", "w_ukv", "w_out", "ffn_norm",
        "dense_w1", "dense_w3", "dense_w2", "w_router", "moe_w1", "moe_w3", "moe_w2"]


def kernel(**inputs):
    import concourse.bacc as _bacc
    from concourse.bass_utils import run_bass_kernel_spmd as _run

    nc = _bacc.Bacc("TRN2", target_bir_lowering=False, num_devices=1)
    arrays = {n: np.ascontiguousarray(inputs[n]) for n in _INS}
    arrays["final_norm"] = np.ascontiguousarray(inputs["final_norm"]).reshape(1, D)
    arrays["rel_rev"] = np.ascontiguousarray(np.asarray(inputs["rel_bias"])[:, :, ::-1]).reshape(DEPTH * HEADS, 2 * REL + 1)
    arrays["const"] = _constants()
    t = {n: nc.dram_tensor(f"in_{n}", a.shape, mybir.dt.from_np(a.dtype), kind="ExternalInput").ap() for n, a in arrays.items()}
    out = nc.dram_tensor("out_y", (1, SEQ, D), F32, kind="ExternalOutput").ap()
    build(nc, t, out)
    r = _run(nc, [{f"in_{n}": a for n, a in arrays.items()}], core_ids=[0])
    return r.results[0]["out_y"]
```

```python
from contextlib import ExitStack

import concourse.bass as bass
import numpy as np
from concourse import mybir

F32 = mybir.dt.float32
F32R = mybir.dt.float32r
I32 = mybir.dt.int32
ALU = mybir.AluOpType
ACT = mybir.ActivationFunctionType
AX = mybir.AxisListType

P = 128
D = 1024
SEQ = 256
TB = SEQ // P
DC = D // P
DEPTH = 2
Q_LORA, KV_LORA, ROPE = 384, 256, 32
LATENT = Q_LORA + KV_LORA
LC = LATENT // P
QC = Q_LORA // P
HEADS, HD, NOPE = 8, 64, 64
QK_MLA = NOPE + ROPE
CA = HEADS * HD
IN_DIM = LATENT + ROPE + 3 * CA
CA_Q, CA_K, CA_V = LATENT + ROPE, LATENT + ROPE + CA, LATENT + ROPE + 2 * CA
HALF = ROPE // 2
CHUNK = 64
REL = 128
FFN = 3584
EXPERTS = 8
EPS = 1e-6
NEG = -1e30

TILE = 2048
N_IN = 4
REST = IN_DIM - N_IN * 512
ATTN_TILES = 2 * N_IN + 1 + 2 + 1 + 4
UNIT = 512
UNITS = FFN // UNIT
UNIT_TILES = 6
FFN_TILES = UNIT_TILES * UNITS
RAW, HI, LO = 6, 3, 3
LEAD = 3
HEAD_STEPS = 2 * HEADS
TURNS = HEADS // 2 + HEADS
W_OUT_ORDER = [(0, 1), (0, 0), (1, 0), (1, 1)]
SCORES = P + SEQ
NORMS = 5
PERIOD = 3 * P
PASS_SLOTS = P

C_ID, C_MASK, C_TRI, C_ONE, C_IOTA = 0, P, P + SCORES, 2 * P + SCORES, 3 * P + SCORES
C_COS = C_IOTA + P
C_SIN = C_COS + TB * HALF
C_ALL = C_SIN + TB * HALF

FIRST_TILE = {"attn0": 0, "ffn0": ATTN_TILES, "attn1": ATTN_TILES + FFN_TILES,
              "moe": 2 * ATTN_TILES + FFN_TILES}


def build(nc, t, out):
    with ExitStack() as ctx:
        def sb(name, shape, dt=F32):
            return ctx.enter_context(nc.sbuf_tensor(name, shape, dt))

        def sem(name):
            return ctx.enter_context(nc.semaphore(name))

        raw = sb("raw", [P, RAW, TILE])
        w_hi = sb("w_hi", [P, HI, TILE], F32R)
        w_lo = sb("w_lo", [P, LO, TILE], F32R)
        x = sb("x", [P, TB, D])
        xn = sb("xn", [P, TB, D])
        xT_hi = sb("xT_hi", [P, DC, SEQ], F32R)
        xT_lo = sb("xT_lo", [P, DC, SEQ], F32R)
        z = sb("z", [P, TB, IN_DIM])
        uT_hi = sb("uT_hi", [P, LC, SEQ], F32R)
        uT_lo = sb("uT_lo", [P, LC, SEQ], F32R)
        k_mla = sb("k_mla", [P, TB, HEADS, QK_MLA])
        v_mla = sb("v_mla", [P, TB, HEADS * HD])
        bias = sb("bias", [P, HEADS, SCORES])
        const = sb("const", [P, C_ALL])
        gain = sb("gain", [P, D])
        lat_gain = sb("lat_gain", [P, LATENT])
        qkT = sb("qkT", [P, 2, 2 * SEQ])
        s_sb = sb("s_sb", [P, 3, SCORES])
        pT = sb("pT", [P, 2, SCORES])
        rot = sb("rot", [P, 4, P])
        neg_max = sb("neg_max", [P, 3, TB])
        p_sum = sb("p_sum", [P, 3, TB])
        p_inv = sb("p_inv", [P, 3, TB])
        n_ss = sb("n_ss", [P, 2, TB])
        n_sum = sb("n_sum", [P, TB])
        n_ms = sb("n_ms", [P, TB])
        n_sd = sb("n_sd", [P, TB])
        n_inv = sb("n_inv", [P, NORMS, TB])
        l_ss = sb("l_ss", [P, 4])
        l_ms = sb("l_ms", [P, 4])
        l_sd = sb("l_sd", [P, 4])
        l_inv = sb("l_inv", [P, 4])
        ext = sb("ext", [DEPTH * HEADS, PERIOD])
        wr = sb("wr", [P, DC, EXPERTS])
        wr_parts = sb("wr_parts", [P, DC, 2, EXPERTS], F32R)
        rt = sb("rt", [P, 8, TB, EXPERTS])
        r1 = sb("r1", [P, 8, TB])
        chosen = sb("chosen", [P, TB, EXPERTS + 1])
        gates = sb("gates", [P, TB, EXPERTS + 1])
        pos = sb("pos", [P, TB, EXPERTS + 1])
        full = sb("full", [P, 2])
        full_i = sb("full_i", [P, 1], I32)
        ps = ctx.enter_context(nc.psum_tensor("ps", [P, 8, 512], F32))
        ext_dram = nc.dram_tensor("ext_dram", [DEPTH * HEADS, P * PERIOD], F32, kind="Internal").ap()

        ident = const[:, C_ID:C_ID + P]
        mask = const[:, C_MASK:C_MASK + SCORES]
        tri = const[:, C_TRI:C_TRI + P]
        ones = const[:, C_ONE:C_ONE + P]
        iota = const[:, C_IOTA:C_IOTA + P]
        cos = const[:, C_COS:C_SIN].rearrange("p (b j) -> p b j", b=TB)
        sin = const[:, C_SIN:C_ALL].rearrange("p (b j) -> p b j", b=TB)
        q_mla = xn[:, :, 0:HEADS * QK_MLA]
        z_flat = z[:, :, :].rearrange("p b n -> p (b n)")
        silu = z_flat[:, 0:2 * UNIT].rearrange("p (b n) -> p b n", b=TB)
        hid = z_flat[:, 2 * UNIT:4 * UNIT].rearrange("p (b n) -> p b n", b=TB)
        junk = z_flat[:, 0:4 * UNIT].rearrange("p (h b n) -> p h b n", h=2, b=TB)
        y_hi = [a[:, 0:4, P:SEQ] for a in (uT_hi, xT_hi)]
        y_lo = [a[:, 0:4, P:SEQ] for a in (uT_lo, xT_lo)]
        pick = z_flat[:, 6 * UNIT:6 * UNIT + SEQ].rearrange("p (b s) -> p b s", b=TB)
        pickT = uT_hi[:, LC - 1, :]

        landed = [sem(f"landed{i}") for i in range(RAW)]
        hi_ready = sem("hi_ready")
        lo_ready = sem("lo_ready")
        used = sem("used")
        ident_in = sem("ident_in")
        const_in = sem("const_in")
        x_in = [sem(f"x_in{h}") for h in range(2)]
        gain_in = sem("gain_in")
        lat_gain_in = sem("lat_gain_in")
        rel_in = sem("rel_in")
        router_in = sem("router_in")
        ext_done = sem("ext_done")
        ext_out = sem("ext_out")
        bias_in = sem("bias_in")
        bias_ready = sem("bias_ready")
        w_out_first = sem("w_out_first")
        x_updated = sem("x_updated")
        y_half = sem("y_half")
        xg_ready = sem("xg_ready")
        xg_last = sem("xg_last")
        norm_inv = sem("norm_inv")
        norm_ss = sem("norm_ss")
        norm_ms = sem("norm_ms")
        norm_sd = sem("norm_sd")
        xn_ready = sem("xn_ready")
        xn_out0 = sem("xn_out0")
        xn_out1 = sem("xn_out1")
        lat_ss = sem("lat_ss")
        lat_ms = sem("lat_ms")
        lat_sd = sem("lat_sd")
        lat_ready = sem("lat_ready")
        tr_done = sem("tr_done")
        tr_hi = sem("tr_hi")
        tr_lo = sem("tr_lo")
        z_out = sem("z_out")
        lt_done = sem("lt_done")
        lt_hi = sem("lt_hi")
        lt_lo = sem("lt_lo")
        q_out = sem("q_out")
        kv_out = sem("kv_out")
        k_roped = sem("k_roped")
        q_products = sem("q_products")
        q_roped = sem("q_roped")
        qk_done = sem("qk_done")
        qk_out = sem("qk_out")
        sc_done = sem("sc_done")
        sc_out = sem("sc_out")
        max_done = sem("max_done")
        exp_done = sem("exp_done")
        p_inverted = sem("p_inverted")
        p_ready = sem("p_ready")
        pT_done = sem("pT_done")
        pT_out = sem("pT_out")
        o_done = sem("o_done")
        o_hi = sem("o_hi")
        o_lo = sem("o_lo")
        silu_done = sem("silu_done")
        hid_done = sem("hid_done")
        ht_done = sem("ht_done")
        ht_hi = sem("ht_hi")
        ht_lo = sem("ht_lo")
        rw_hi = sem("rw_hi")
        rw_lo = sem("rw_lo")
        logit_done = sem("logit_done")
        gate_exp_in = sem("gate_exp_in")
        gate_exp = sem("gate_exp")
        chosen_done = sem("chosen_done")
        pos_done = sem("pos_done")
        counted = sem("counted")
        routed = sem("routed")
        pos_moved = sem("pos_moved")
        pick_done = sem("pick_done")
        ga_done = sem("ga_done")
        ga_hi = sem("ga_hi")
        ga_lo = sem("ga_lo")
        st_done = sem("st_done")
        st_out = sem("st_out")
        y_hi_out = sem("y_hi_out")
        y_lo_out = sem("y_lo_out")
        sct_done = sem("sct_done")
        x_acc = sem("x_acc")
        dve_step = sem("dve_step")
        out_stored = sem("out_stored")

        def width(n):
            for base in (FIRST_TILE["attn0"], FIRST_TILE["attn1"]):
                k = n - base
                if 0 <= k < ATTN_TILES:
                    if k == 2 * N_IN:
                        return DC * REST
                    if k in (2 * N_IN + 1, 2 * N_IN + 2):
                        return QC * Q_LORA
            return TILE

        def hi_of(n, cols):
            w = width(n)
            return w_hi[:, n % HI, 0:w].rearrange("p (k n) -> p k n", n=cols)

        def lo_of(n, cols):
            w = width(n)
            return w_lo[:, n % LO, 0:w].rearrange("p (k n) -> p k n", n=cols)

        def load(eng, n, step, src):
            if n >= RAW:
                eng.wait_ge(lo_ready, n - RAW + 1 + UNIT_TILES * step)
            shape = src.shape
            dst = raw[:, n % RAW, 0:width(n)].rearrange("p (k n) -> p k n", n=shape[2])
            eng.dma_start(dst, src).then_inc(landed[n % RAW], 16)

        def round_hi(act, n, step=0):
            act.wait_ge(landed[n % RAW], 16 * (n // RAW + 1) + 16 * (UNIT_TILES // RAW) * step)
            if n >= HI:
                act.wait_ge(used, n - HI + 1 + UNIT_TILES * step)
            w = width(n)
            nc.scalar.activation(w_hi[:, n % HI, 0:w], raw[:, n % RAW, 0:w], ACT.Copy).then_inc(hi_ready, 1)

        def split_lo(dve, n, step=0):
            dve.wait_ge(hi_ready, n + 1 + UNIT_TILES * step)
            if n >= LO:
                dve.wait_ge(used, n - LO + 1 + UNIT_TILES * step)
            w = width(n)
            nc.vector.tensor_tensor(w_lo[:, n % LO, 0:w], raw[:, n % RAW, 0:w],
                                    w_hi[:, n % HI, 0:w].bitcast(F32), ALU.subtract).then_inc(lo_ready, 1)

        def multiplied(eng, n, step=0):
            eng.wait_ge(used, n + 1 + UNIT_TILES * step)

        def product(out_ap, x_hi, x_lo, y_hi, y_lo, start, stop):
            nc.tensor.matmul(out_ap, x_hi, y_hi, start=start, stop=False)
            nc.tensor.matmul(out_ap, x_hi, y_lo, start=False, stop=False)
            return nc.tensor.matmul(out_ap, x_lo, y_hi, start=False, stop=stop)

        def bank(b, n=512):
            return ps[:, b, 0:n]

        half_cols = [slice(0, D // 2), slice(D // 2, D)]
        tok = [slice(b * P, (b + 1) * P) for b in range(TB)]
        HEAD_ORDER = [(True, h) for h in range(HEADS)] + [(False, h) for h in range(HEADS)]

        def head_dims(ca):
            return HD if ca else QK_MLA

        def turn_of(i):
            layer, s = divmod(i, HEAD_STEPS)
            return TURNS * layer + (s // 2 if s < HEADS else s - HEADS // 2)

        def starts_turn(s):
            return s >= HEADS or s % 2 == 0

        def heads_through(turn):
            layer, g = divmod(turn, TURNS)
            return HEAD_STEPS * layer + (2 * g + 2 if g < HEADS // 2 else g + HEADS // 2 + 1)

        EXPERT_STEPS = UNITS
        MOE = FIRST_TILE["moe"]
        DENSE_UNITS = TB * UNITS

        def passes(emit, eng, p):
            it0 = p * EXPERTS
            emit(eng, it0, True, False)
            with eng.Fori(it0 + 1, it0 + EXPERTS - 1) as it:
                emit(eng, it, False, False)
            emit(eng, it0 + EXPERTS - 1, False, True)

        block = ctx.enter_context(nc.Block())

        @block.sync
        def _(sp):
            x_rows = t["x"].rearrange("a (b p) d -> p (a b) d", p=P)
            sp.dma_start(x[:, :, half_cols[0]], x_rows[:, :, half_cols[0]]).then_inc(x_in[0], 16)
            sp.dma_start(ident, t["const"][:, C_ID:C_ID + P]).then_inc(ident_in, 16)
            sp.dma_start(x[:, :, half_cols[1]], x_rows[:, :, half_cols[1]]).then_inc(x_in[1], 16)

            def attn_tiles(layer):
                n = FIRST_TILE[f"attn{layer}"]
                w_in = t["w_in"][layer].rearrange("(k p) n -> p k n", p=P)
                for g in range(N_IN):
                    for half in range(2):
                        load(sp, n, 0, w_in[:, 4 * half:4 * half + 4, 512 * g:512 * g + 512])
                        n += 1
                        if n == LEAD:
                            sp.dma_start(const[:, P:C_ALL], t["const"][:, P:C_ALL]).then_inc(const_in, 16)
                load(sp, n, 0, w_in[:, :, 512 * N_IN:IN_DIM])
                w_uq = t["w_uq"][layer].rearrange("(k p) n -> p k n", p=P)
                for j in range(2):
                    load(sp, n + 1 + j, 0, w_uq[:, :, Q_LORA * j:Q_LORA * (j + 1)])
                load(sp, n + 3, 0, t["w_ukv"][layer].rearrange("(k p) n -> p k n", p=P))
                w_out = t["w_out"][layer].rearrange("(k p) n -> p k n", p=P)
                for i, (g, half) in enumerate(W_OUT_ORDER):
                    load(sp, n + 4 + i, 0, w_out[:, 4 * half:4 * half + 4, 512 * g:512 * g + 512])

            def up_tiles(n, step, w, f):
                w = w.rearrange("(k p) n -> p k n", p=P)
                for half in range(2):
                    load(sp, n + half, step, w[:, 4 * half:4 * half + 4, bass.ds(f * UNIT, UNIT)])

            def down_tiles(n, step, w, f):
                w = w.rearrange("(u k p) n -> u p k n", p=P, k=4)
                for half in range(2):
                    src = w[bass.ds(f, 1), :, 2 * half:2 * half + 2, :]
                    load(sp, n + half, step, src.rearrange("u p k n -> p (u k) n"))

            def ffn_tiles(n, step, w1, w3, w2):
                up_tiles(n, step, w1, 0)
                up_tiles(n + 2, step, w3, 0)
                with sp.Fori(0, UNITS - 1) as f:
                    up_tiles(n + 4, step + f, w1, f + 1)
                    up_tiles(n + 6, step + f, w3, f + 1)
                    down_tiles(n + 8, step + f, w2, f)
                down_tiles(n + 4, step + UNITS - 1, w2, UNITS - 1)

            def expert_tiles(it, e):
                def of(name):
                    return t[name][0, bass.ds(e, 1)].rearrange("e a b -> (e a) b")
                ffn_tiles(MOE, EXPERT_STEPS * it, of("moe_w1"), of("moe_w3"), of("moe_w2"))

            attn_tiles(0)
            ffn_tiles(FIRST_TILE["ffn0"], 0, t["dense_w1"][0], t["dense_w3"][0], t["dense_w2"][0])
            attn_tiles(1)
            with sp.Fori(0, EXPERTS) as e:
                expert_tiles(e, e)
            sp.wait_ge(routed, 1)
            more = sp.value_load(full_i[0:1, 0:1], min_val=0, max_val=1)
            with sp.If(more == 1):
                with sp.Fori(0, EXPERTS) as e:
                    expert_tiles(e + EXPERTS, e)
                sp.wait_ge(x_acc, 2 * 4 * EXPERTS)
            for b in range(TB):
                sp.wait_ge((xn_out0, xn_out1)[b], 1)
                sp.dma_start(out.rearrange("a (b p) d -> p (a b) d", p=P)[:, b, :], xn[:, b, :]).then_inc(out_stored, 16)
            sp.wait_ge(out_stored, 16 * TB)

        @block.gpsimd
        def _(pool):
            def load_gain(k):
                src = [t["attn_norm"][0:1], t["ffn_norm"][0:1], t["attn_norm"][1:2], t["ffn_norm"][1:2], t["final_norm"]][k]
                if k:
                    pool.wait_ge(xg_ready, 4 * k)
                pool.dma_start(gain[:, :], src.to_broadcast([P, D])).then_inc(gain_in, 16)

            def load_lat_gain(layer):
                if layer:
                    pool.wait_ge(lat_ready, 4 * layer)
                pool.dma_start(lat_gain[:, 0:Q_LORA], t["q_norm"][layer:layer + 1].to_broadcast([P, Q_LORA])).then_inc(lat_gain_in, 16)
                pool.dma_start(lat_gain[:, Q_LORA:LATENT], t["kv_norm"][layer:layer + 1].to_broadcast([P, KV_LORA])).then_inc(lat_gain_in, 16)

            def load_bias(layer):
                if layer:
                    pool.wait_ge(sc_out, HEAD_STEPS * layer)
                for first, base, n in ((0, 2 * REL - 1, P), (P, REL - 1, SEQ)):
                    e = ext_dram[layer * HEADS:(layer + 1) * HEADS, base:base + 1]
                    src = bass.AP(e.tensor, e.offset, [[PERIOD - 1, P], [P * PERIOD, HEADS], [1, n]])
                    pool.dma_start(bias[:, :, first:first + n], src).then_inc(bias_in, 16)
                pool.wait_ge(bias_in, 32 * (layer + 1))
                for diagonal in (0, 2 * P):
                    nc.gpsimd.memset(bias[0:CHUNK, :, diagonal + CHUNK:diagonal + P], NEG).then_inc(bias_ready, 1)

            def rotate_queries(layer):
                pool.wait_ge(const_in, 16)
                pool.wait_ge(k_roped, 2 * (layer + 1))
                pool.wait_ge(q_out, 4 * (layer + 1))
                for b in range(TB):
                    q = q_mla[:, b, :].rearrange("p (h c) -> p h c", c=QK_MLA)[:, :, NOPE:QK_MLA]
                    x1, x2 = q[:, :, 0:HALF], q[:, :, HALF:ROPE]
                    c = cos[:, b:b + 1, :].to_broadcast([P, HEADS, HALF])
                    s = sin[:, b:b + 1, :].to_broadcast([P, HEADS, HALF])
                    parts = [rot[:, i, :].rearrange("p (h j) -> p h j", h=HEADS) for i in range(4)]
                    for i, (a, w) in enumerate(((x1, c), (x2, s), (x1, s), (x2, c))):
                        nc.gpsimd.tensor_tensor(parts[i], a, w, ALU.mult).then_inc(q_products, 1)
                    pool.wait_ge(q_products, 4 * (TB * layer + b + 1))
                    nc.gpsimd.tensor_tensor(x1, parts[0], parts[1], ALU.subtract).then_inc(q_roped, 1)
                    nc.gpsimd.tensor_tensor(x2, parts[2], parts[3], ALU.add).then_inc(q_roped, 1)
                    pool.wait_ge(q_roped, 2 * (TB * layer + b + 1))

            load_gain(0)
            load_lat_gain(0)
            pool.dma_start(ext[:, REL - 1:PERIOD], t["rel_rev"][:, 0:2 * REL + 1]).then_inc(rel_in, 16)
            pool.dma_start(wr[:, :, :], t["w_router"][0].rearrange("(k p) e -> p k e", p=P)).then_inc(router_in, 16)
            pool.wait_ge(rel_in, 16)
            nc.gpsimd.tensor_copy(ext[:, 0:REL - 1], ext[:, REL - 1:REL].to_broadcast([DEPTH * HEADS, REL - 1])).then_inc(ext_done, 1)
            pool.wait_ge(ext_done, 1)
            rows = bass.AP(ext[:, :].tensor, ext[:, :].offset, [ext[:, :].ap[0], [0, P], [1, PERIOD]])
            pool.dma_start(ext_dram.rearrange("h (r d) -> h r d", r=P), rows).then_inc(ext_out, 16)
            pool.wait_ge(ext_out, 16)
            load_bias(0)
            load_gain(1)
            rotate_queries(0)
            load_gain(2)
            load_lat_gain(1)
            load_bias(1)
            load_gain(3)
            rotate_queries(1)
            load_gain(4)

        @block.scalar
        def _(act):
            def squares(k, h, acc=0):
                if k == 0:
                    act.wait_ge(x_in[h], 16)
                elif k < NORMS - 1:
                    act.wait_ge(x_updated, 4 * (k - 1) + TB * (h + 1))
                for b in range(TB):
                    if k == NORMS - 1:
                        act.wait_ge(x_acc, acc + TB * h + b + 1)
                    nc.scalar.activation(junk[:, h, b, :], x[:, b, half_cols[h]], ACT.Square,
                                         accum_out=n_ss[:, h, b:b + 1]).then_inc(norm_ss, 1)

            def root(k):
                act.wait_ge(norm_ms, k + 1)
                nc.scalar.activation(n_sd[:, :], n_ms[:, :], ACT.Sqrt).then_inc(norm_sd, 1)

            def transposed_hi(k, h):
                for g in (2 * h, 2 * h + 1):
                    act.wait_ge(tr_done, 4 * k + g + 1)
                    nc.scalar.activation(xT_hi[:, 2 * g:2 * g + 2, :], bank(4 * (k % 2) + g), ACT.Copy).then_inc(tr_hi, 1)

            def attention(layer):
                n0 = FIRST_TILE[f"attn{layer}"]
                k_norm = 2 * layer

                def z_copy(g):
                    if g == 0:
                        act.wait_ge(norm_inv, k_norm + 1)
                    multiplied(act, n0 + min(2 * g + 1, 2 * N_IN))
                    for b in range(TB):
                        w = 512 if g < N_IN else REST
                        nc.scalar.activation(z[:, b, 512 * g:512 * g + w], bank(4 + 2 * (g % 2) + b, w),
                                             ACT.Copy, scale=n_inv[:, k_norm, b:b + 1]).then_inc(z_out, 1)

                def latents_hi():
                    for g in range(3):
                        act.wait_ge(lt_done, 3 * layer + g + 1)
                        m = min(2, LC - 2 * g)
                        nc.scalar.activation(uT_hi[:, 2 * g:2 * g + m, :], bank(g, m * SEQ), ACT.Copy).then_inc(lt_hi, 1)

                n = n0 + LEAD
                for g in range(N_IN):
                    for half in range(2):
                        round_hi(act, n)
                        n += 1
                        if (g, half) == (N_IN - 1, 0):
                            latents_hi()
                    z_copy(g)
                    if g == 1:
                        act.wait_ge(z_out, 10 * layer + 4)
                        for b in range(TB):
                            for j, (a, c) in enumerate(((0, Q_LORA), (Q_LORA, LATENT))):
                                nc.scalar.activation(xn[:, b, a:c], z[:, b, a:c], ACT.Square,
                                                     accum_out=l_ss[:, 2 * j + b:2 * j + b + 1]).then_inc(lat_ss, 1)
                    if g == 2:
                        act.wait_ge(lat_ms, layer + 1)
                        nc.scalar.activation(l_sd[:, :], l_ms[:, :], ACT.Sqrt).then_inc(lat_sd, 1)
                def kv_copy(g):
                    for b in range(TB):
                        kv = bank(4 + 2 * g + b).rearrange("p (h c) -> p h c", c=2 * HD)
                        nc.scalar.activation(k_mla[:, b, 4 * g:4 * g + 4, 0:NOPE], kv[:, :, 0:HD], ACT.Copy)
                        v = v_mla[:, b, :].rearrange("p (h c) -> p h c", c=HD)
                        nc.scalar.activation(v[:, 4 * g:4 * g + 4, :], kv[:, :, HD:2 * HD], ACT.Copy).then_inc(kv_out, 1)

                def head_step(s):
                    i = HEAD_STEPS * layer + s
                    if s < HEAD_STEPS and starts_turn(s):
                        g = turn_of(i)
                        act.wait_ge(qk_done, g + 1)
                        if g >= 2:
                            act.wait_ge(sc_done, heads_through(g - 2))
                        d = P if s < HEADS else QK_MLA
                        nc.scalar.activation(qkT[0:d, g % 2, :], ps[0:d, g % 2, :], ACT.Copy).then_inc(qk_out, 1)
                    if 2 <= s < HEAD_STEPS + 2:
                        j = i - 2
                        act.wait_ge(max_done, j + 1)
                        for b, (a, c) in enumerate(((0, P), (P, SCORES))):
                            ins = nc.scalar.activation(s_sb[:, j % 3, a:c], s_sb[:, j % 3, a:c], ACT.Exp,
                                                       bias=neg_max[:, j % 3, b:b + 1], accum_out=p_sum[:, j % 3, b:b + 1])
                        ins.then_inc(exp_done, 1)
                    if s == 3:
                        multiplied(act, n0 + 2 * N_IN + 3)
                        kv_copy(0)
                    if s == 4:
                        kv_copy(1)
                    if 3 <= s < HEAD_STEPS + 3:
                        j = i - 3
                        act.wait_ge(pT_done, j + 1)
                        if j >= 2:
                            act.wait_ge(o_done, j - 1)
                        nc.scalar.activation(pT[:, j % 2, :], bank(4 + j % 2, SCORES), ACT.Copy).then_inc(pT_out, 1)
                    if s >= 4:
                        j = i - 4
                        ca, h = HEAD_ORDER[s - 4]
                        if h % 2:
                            act.wait_ge(o_done, j + 1)
                            nc.scalar.activation(xT_hi[:, (HEADS * ca + h) // 2, :], bank(6 + j // 2 % 2, SEQ), ACT.Copy).then_inc(o_hi, 1)

                z_copy(N_IN)
                round_hi(act, n)
                n += 1
                head_step(0)
                nc.scalar.activation(l_sd[:, :], l_ms[:, :], ACT.Exp)
                for j in range(2):
                    multiplied(act, n0 + 2 * N_IN + 1 + j)
                    for b in range(TB):
                        nc.scalar.activation(q_mla[:, b, Q_LORA * j:Q_LORA * (j + 1)], bank(4 + 2 * j + b, Q_LORA),
                                             ACT.Copy).then_inc(q_out, 1)
                    head_step(j + 1)
                    round_hi(act, n)
                    n += 1
                for s in range(3, HEAD_STEPS + 4):
                    head_step(s)
                next_norm = k_norm + 1
                for j in range(3):
                    round_hi(act, n + j)
                squares(next_norm, 0)
                round_hi(act, n + 3)
                transposed_hi(next_norm, 0)
                round_hi(act, n + 4)
                squares(next_norm, 1)
                transposed_hi(next_norm, 1)
                root(next_norm)

            def ffn(n, step, u0, blocks, cut=False, mid=None, xtra_end=None, k_norm=None, ending=None):
                def silu_of(f, st=None):
                    multiplied(act, n + 1 if st is None else n + 5, step if st is None else st)
                    for b in range(blocks):
                        if not _is_zero(u0, f):
                            act.wait_ge(hid_done, u0 + blocks * f + b + 1 - blocks)
                        scale = 1.0 if k_norm is None else n_inv[:, k_norm, b:b + 1]
                        nc.scalar.activation(silu[:, b, :], bank(b), ACT.Silu, scale=scale).then_inc(silu_done, 1)

                def hidden_hi(f):
                    for b in range(blocks):
                        act.wait_ge(ht_done, u0 + blocks * f + b + 1)
                        nc.scalar.activation(uT_hi[:, 0:4, tok[b]],
                                             bank(2 + b).rearrange("p (k s) -> p k s", s=P), ACT.Copy).then_inc(ht_hi, 1)

                round_hi(act, n + 3, step)
                if k_norm is not None:
                    act.wait_ge(norm_inv, k_norm + 1)
                silu_of(0)
                for j in (4, 5, 6):
                    round_hi(act, n + j, step)
                hidden_hi(0)

                def unit(f, st, last):
                    round_hi(act, n + 7, st)
                    round_hi(act, n + 8, st)
                    silu_of(f, st)
                    for j in (9, 10, 11):
                        round_hi(act, n + j, st)
                    if not last:
                        round_hi(act, n + 12, st)
                    hidden_hi(f)
                    if last and not cut:
                        round_hi(act, n + 12, st)

                with act.Fori(1, UNITS - 1) as f:
                    unit(f, step + f - 1, False)
                if mid:
                    mid()
                unit(UNITS - 1, step + UNITS - 2, True)
                if xtra_end:
                    xtra_end()
                if ending:
                    ending(lambda j: round_hi(act, n + 7 + j, step + UNITS - 1))
                elif not cut:
                    round_hi(act, n + 7, step + UNITS - 1)
                    round_hi(act, n + 8, step + UNITS - 1)

            def gathered_hi(it):
                for g in range(2):
                    act.wait_ge(ga_done, 2 * it + g + 1)
                    nc.scalar.activation(xT_hi[:, 4 * g:4 * g + 4, 0:P], bank(1 + 2 * g).rearrange("p (k s) -> p k s", s=P),
                                         ACT.Copy).then_inc(ga_hi, 1)

            def expert(act, it, first, last):
                def pick_copy():
                    if not first:
                        act.wait_ge(sct_done, 4 * it)
                    act.wait_ge(st_done, it + 1)
                    nc.scalar.activation(pickT, ps[:, 6, 0:SEQ], ACT.Copy).then_inc(st_out, 1)

                def gather_next():
                    if not last:
                        gathered_hi(it + 1)

                ffn(MOE, EXPERT_STEPS * it, DENSE_UNITS + UNITS * it, 1, cut=last, mid=pick_copy, xtra_end=gather_next)
                if last:
                    nc.scalar.activation(n_sd[:, :], n_ms[:, :], ACT.Sqrt)
                act.wait_ge(y_half, it + 2)
                if not first:
                    act.wait_ge(sct_done, 4 * it)
                for g in range(2):
                    if g == 1:
                        multiplied(act, MOE + 5, EXPERT_STEPS * it + UNITS - 1)
                    nc.scalar.activation(y_hi[g], bank(4 + g).rearrange("p (k s) -> p k s", s=P), ACT.Copy).then_inc(y_hi_out, 1)

            def renew(round_next):
                squares(2, 0)
                transposed_hi(2, 0)
                round_next(0)
                round_next(1)
                squares(2, 1)
                transposed_hi(2, 1)
                root(2)

            transposed_hi(0, 0)
            round_hi(act, 0)
            transposed_hi(0, 1)
            round_hi(act, 1)
            squares(0, 0)
            squares(0, 1)
            round_hi(act, 2)
            root(0)
            attention(0)
            ffn(FIRST_TILE["ffn0"], 0, 0, TB, k_norm=1, ending=renew)
            act.wait_ge(router_in, 16)
            nc.scalar.activation(wr_parts[:, :, 0, :], wr[:, :, :], ACT.Copy).then_inc(rw_hi, 1)
            attention(1)
            act.wait_ge(norm_inv, 4)
            for b in range(TB):
                nc.scalar.activation(xn[:, b, :], xn[:, b, :], ACT.Copy, scale=n_inv[:, 3, b:b + 1]).then_inc(xn_ready, 1)
            act.wait_ge(gate_exp_in, 1)
            nc.scalar.activation(r1[:, 5, :], r1[:, 4, :], ACT.Exp).then_inc(gate_exp, 1)
            nc.scalar.activation(n_sd[:, :], n_ms[:, :], ACT.Silu)
            gathered_hi(0)
            passes(expert, act, 0)
            act.wait_ge(routed, 1)
            more = act.value_load(full_i[0:1, 0:1], min_val=0, max_val=1)
            with act.If(more == 1):
                for n in range(LEAD):
                    round_hi(act, MOE + n, EXPERT_STEPS * EXPERTS)
                gathered_hi(EXPERTS)
                passes(expert, act, 1)
                for h in range(2):
                    squares(4, h, 4 * (2 * EXPERTS - 1))
            with act.If(more == 0):
                for h in range(2):
                    squares(4, h, 4 * (EXPERTS - 1))
            root(4)
            act.wait_ge(xg_last, 1)
            act.wait_ge(norm_inv, 5)
            nc.scalar.activation(xn[:, 1, :], xn[:, 1, :], ACT.Copy, scale=n_inv[:, 4, 1:2]).then_inc(xn_out1, 1)

        @block.vector
        def _(dve):
            chain = [0]

            def link(ins):
                chain[0] += 1
                ins.then_inc(dve_step, 1)
                dve.wait_ge(dve_step, chain[0])

            def inverse_rms(k, meanwhile=None):
                dve.wait_ge(norm_ss, 2 * TB * (k + 1))
                link(nc.vector.tensor_tensor(n_sum[:, :], n_ss[:, 0, :], n_ss[:, 1, :], ALU.add))
                nc.vector.tensor_scalar(n_ms[:, :], n_sum[:, :], 1.0 / D, EPS, ALU.mult, ALU.add).then_inc(norm_ms, 1)
                if meanwhile:
                    meanwhile()
                dve.wait_ge(norm_sd, k + 1)
                nc.vector.reciprocal(n_inv[:, k, :], n_sd[:, :]).then_inc(norm_inv, 1)

            def x_times_gain(k, h, b):
                nc.vector.tensor_tensor(xn[:, b, half_cols[h]], x[:, b, half_cols[h]], gain[:, half_cols[h]],
                                        ALU.mult).then_inc(xg_ready, 1)

            def update(k, h, blocks=range(TB)):
                first_bank = 0 if k % 2 else 4
                for b in blocks:
                    nc.vector.tensor_tensor(x[:, b, half_cols[h]], bank(first_bank + 2 * h + b), x[:, b, half_cols[h]],
                                            ALU.add).then_inc(x_updated, 1)
                dve.wait_ge(gain_in, 16 * (k + 1))
                for b in blocks:
                    dve.wait_ge(x_updated, 4 * (k - 1) + TB * h + b + 1)
                    x_times_gain(k, h, b)

            def transposed_lo(k, h):
                for g in (2 * h, 2 * h + 1):
                    dve.wait_ge(tr_hi, 4 * k + g + 1)
                    nc.vector.tensor_tensor(xT_lo[:, 2 * g:2 * g + 2, :], bank(4 * (k % 2) + g).rearrange("p (k s) -> p k s", s=SEQ),
                                            xT_hi[:, 2 * g:2 * g + 2, :].bitcast(F32), ALU.subtract).then_inc(tr_lo, 1)

            def rotate(v, shape, out1, out2, done):
                v1, v2 = v[..., 0:HALF], v[..., HALF:ROPE]
                m = int(np.prod(shape))
                c, s = cos, sin
                if len(shape) == 3:
                    c = bass.AP(cos.tensor, cos.offset, [cos.ap[0], cos.ap[1], [0, shape[1]], cos.ap[2]])
                    s = bass.AP(sin.tensor, sin.offset, [sin.ap[0], sin.ap[1], [0, shape[1]], sin.ap[2]])
                    parts = [rot[:, i, 0:m].rearrange("p (b h j) -> p b h j", b=shape[0], h=shape[1]) for i in range(4)]
                else:
                    parts = [rot[:, i, 0:m].rearrange("p (b j) -> p b j", b=shape[0]) for i in range(4)]
                for i, (a, w) in enumerate(((v1, c), (v2, s), (v1, s), (v2, c))):
                    ins = nc.vector.tensor_tensor(parts[i], a, w, ALU.mult)
                link(ins)
                nc.vector.tensor_tensor(out1, parts[0], parts[1], ALU.subtract)
                ins = nc.vector.tensor_tensor(out2, parts[2], parts[3], ALU.add)
                if done is not None:
                    ins.then_inc(done, 1)
                else:
                    link(ins)

            def attention(layer):
                n0 = FIRST_TILE[f"attn{layer}"]
                n = n0 + LEAD

                def latents_lo():
                    for g in range(3):
                        dve.wait_ge(lt_hi, 3 * layer + g + 1)
                        m = min(2, LC - 2 * g)
                        nc.vector.tensor_tensor(uT_lo[:, 2 * g:2 * g + m, :], bank(g, m * SEQ).rearrange("p (k s) -> p k s", s=SEQ),
                                                uT_hi[:, 2 * g:2 * g + m, :].bitcast(F32), ALU.subtract).then_inc(lt_lo, 1)

                for g in range(N_IN + 1):
                    for half in range(2 if g < N_IN else 1):
                        split_lo(dve, n)
                        n += 1
                        if (g, half) == (N_IN - 1, 0):
                            latents_lo()
                    if g == 1:
                        dve.wait_ge(lat_ss, 4 * (layer + 1))
                        nc.vector.tensor_scalar(l_ms[:, 0:2], l_ss[:, 0:2], 1.0 / Q_LORA, EPS, ALU.mult, ALU.add)
                        nc.vector.tensor_scalar(l_ms[:, 2:4], l_ss[:, 2:4], 1.0 / KV_LORA, EPS, ALU.mult, ALU.add).then_inc(lat_ms, 1)
                        k_r = z[:, :, LATENT:LATENT + ROPE]
                        rotate(k_r, (TB, HALF), k_r[..., 0:HALF], k_r[..., HALF:ROPE], None)
                        for b in range(TB):
                            nc.vector.tensor_copy(k_mla[:, b, :, NOPE:QK_MLA],
                                                  z[:, b:b + 1, LATENT:LATENT + ROPE].to_broadcast([P, HEADS, ROPE])).then_inc(k_roped, 1)
                    if g == 2:
                        dve.wait_ge(lat_sd, layer + 1)
                        link(nc.vector.reciprocal(l_inv[:, :], l_sd[:, :]))
                        dve.wait_ge(lat_gain_in, 32 * (layer + 1))
                        for b in range(TB):
                            for j, (a, c) in enumerate(((0, Q_LORA), (Q_LORA, LATENT))):
                                nc.vector.scalar_tensor_tensor(z[:, b, a:c], z[:, b, a:c], l_inv[:, 2 * j + b:2 * j + b + 1],
                                                               lat_gain[:, a:c], ALU.mult, ALU.mult).then_inc(lat_ready, 1)

                def head_step(s):
                    i = HEAD_STEPS * layer + s
                    scored, normed = i - 1, i - 2
                    if s < HEAD_STEPS + 1:
                        ca, h = HEAD_ORDER[s - 1]
                        dve.wait_ge(sc_done, scored + 1)
                        if scored >= 3:
                            dve.wait_ge(pT_done, scored - 2)
                        nc.vector.scalar_tensor_tensor(s_sb[:, scored % 3, :], bank(2 + scored % 2, SCORES), head_dims(ca) ** -0.5,
                                                       bias[:, h, :] if ca else mask, ALU.mult, ALU.add).then_inc(sc_out, 1)
                        dve.wait_ge(sc_out, scored + 1)
                        for b, (a, c) in enumerate(((0, P), (P, SCORES))):
                            ins = nc.vector.tensor_reduce(neg_max[:, scored % 3, b:b + 1], s_sb[:, scored % 3, a:c], AX.X, ALU.max, negate=True)
                        ins.then_inc(max_done, 1)
                    if 2 <= s < HEAD_STEPS + 2:
                        dve.wait_ge(exp_done, normed + 1)
                        nc.vector.reciprocal(p_inv[:, normed % 3, :], p_sum[:, normed % 3, :]).then_inc(p_inverted, 1)
                        dve.wait_ge(p_inverted, normed + 1)
                        for b, (a, c) in enumerate(((0, P), (P, SCORES))):
                            p = s_sb[:, normed % 3, a:c]
                            ins = nc.vector.tensor_scalar(p, p, p_inv[:, normed % 3, b:b + 1], None, ALU.mult)
                        ins.then_inc(p_ready, 1)
                    if s >= 4:
                        j = i - 4
                        ca, h = HEAD_ORDER[s - 4]
                        if h % 2:
                            c = (HEADS * ca + h) // 2
                            dve.wait_ge(o_hi, j // 2 + 1)
                            nc.vector.tensor_tensor(xT_lo[:, c, :], bank(6 + j // 2 % 2, SEQ), xT_hi[:, c, :].bitcast(F32),
                                                    ALU.subtract).then_inc(o_lo, 1)

                dve.wait_ge(bias_ready, 2 * (layer + 1))
                for j in range(2):
                    head_step(j + 1)
                    split_lo(dve, n)
                    n += 1
                for s in range(3, HEAD_STEPS + 4):
                    head_step(s)
                k_norm = 2 * layer + 1
                split_lo(dve, n)
                split_lo(dve, n + 1)
                multiplied(dve, n - 1)
                update(k_norm, 0)
                split_lo(dve, n + 2)
                split_lo(dve, n + 3)
                transposed_lo(k_norm, 0)
                dve.wait_ge(w_out_first, layer + 1)
                update(k_norm, 1, [0])
                multiplied(dve, n + 1)
                update(k_norm, 1, [1])
                transposed_lo(k_norm, 1)
                inverse_rms(k_norm, meanwhile=lambda: split_lo(dve, n + 4))

            def ffn(n, step, u0, blocks, extra=None, cut=False, xtra_end=None, mid=None, k_norm=None, ending=None):
                def hidden(f, st=None):
                    multiplied(dve, n + 3 if st is None else n + 7, step if st is None else st)
                    for b in range(blocks):
                        dve.wait_ge(silu_done, u0 + blocks * f + b + 1)
                        if not _is_zero(u0, f):
                            dve.wait_ge(ht_done, u0 + blocks * f + b + 1 - blocks)
                        if k_norm is None:
                            ins = nc.vector.tensor_tensor(hid[:, b, :], bank(2 + b), silu[:, b, :], ALU.mult)
                        else:
                            ins = nc.vector.scalar_tensor_tensor(hid[:, b, :], bank(2 + b), n_inv[:, k_norm, b:b + 1],
                                                                 silu[:, b, :], ALU.mult, ALU.mult)
                        ins.then_inc(hid_done, 1)

                def hidden_lo(f):
                    for b in range(blocks):
                        dve.wait_ge(ht_hi, u0 + blocks * f + b + 1)
                        nc.vector.tensor_tensor(uT_lo[:, 0:4, tok[b]], bank(2 + b).rearrange("p (k s) -> p k s", s=P),
                                                uT_hi[:, 0:4, tok[b]].bitcast(F32), ALU.subtract).then_inc(ht_lo, 1)

                for j in (3, 4):
                    split_lo(dve, n + j, step)
                hidden(0)
                for j in (5, 6):
                    split_lo(dve, n + j, step)
                hidden_lo(0)
                if extra:
                    extra()

                def unit(f, st, last):
                    for j in (7, 8, 9):
                        split_lo(dve, n + j, st)
                    hidden(f, st)
                    split_lo(dve, n + 10, st)
                    if not (last and cut):
                        split_lo(dve, n + 11, st)
                    if not last:
                        split_lo(dve, n + 12, st)
                    hidden_lo(f)
                    if last:
                        split_lo(dve, n + (11 if cut else 12), st)

                with dve.Fori(1, UNITS - 1) as f:
                    unit(f, step + f - 1, False)
                if mid:
                    mid()
                unit(UNITS - 1, step + UNITS - 2, True)
                if xtra_end:
                    xtra_end()
                if ending:
                    ending(lambda j: split_lo(dve, n + 7 + j, step + UNITS - 1))
                elif not cut:
                    split_lo(dve, n + 7, step + UNITS - 1)
                    split_lo(dve, n + 8, step + UNITS - 1)

            def make_pick(it, p, e):
                for b in range(TB):
                    ins = nc.vector.tensor_scalar(pick[:, b, :], iota, pos[:, b, bass.ds(e, 1)],
                                                  chosen[:, b, bass.ds(e, 1)], ALU.is_equal, ALU.mult)
                ins.then_inc(pick_done, 1)

            def route():
                L, idx, first, left = (rt[:, i] for i in range(4))
                oh1, oh2, tmp = (rt[:, i] for i in range(4, 7))
                io = bass.AP(iota.tensor, iota.offset, [iota.ap[0], [0, TB], [1, EXPERTS]])

                def per_token(i):
                    v = r1[:, i, :]
                    return bass.AP(v.tensor, v.offset, [v.ap[0], v.ap[1], [0, EXPERTS]])

                dve.wait_ge(logit_done, 1)
                for b in range(TB):
                    ins = nc.vector.tensor_scalar(tmp[:, b, :], ps[:, b, EXPERTS:2 * EXPERTS], n_inv[:, 3, b:b + 1], None, ALU.mult)
                link(ins)
                for b in range(TB):
                    ins = nc.vector.scalar_tensor_tensor(L[:, b, :], ps[:, b, 0:EXPERTS], n_inv[:, 3, b:b + 1], tmp[:, b, :],
                                                         ALU.mult, ALU.add)
                link(ins)

                def top(src, value, onehot):
                    link(nc.vector.tensor_reduce(r1[:, value, :], src, AX.X, ALU.max))
                    link(nc.vector.tensor_tensor(tmp, src, per_token(value), ALU.is_equal))
                    link(nc.vector.scalar_tensor_tensor(idx, tmp, -float(EXPERTS), io, ALU.mult, ALU.add))
                    link(nc.vector.tensor_reduce(r1[:, 2, :], idx, AX.X, ALU.min))
                    link(nc.vector.tensor_tensor(onehot, idx, per_token(2), ALU.is_equal))

                top(L, 0, oh1)
                link(nc.vector.scalar_tensor_tensor(left, oh1, -3e38, L, ALU.mult, ALU.add))
                top(left, 1, oh2)
                link(nc.vector.tensor_tensor(chosen[:, :, 0:EXPERTS], oh1, oh2, ALU.add))
                nc.vector.memset(chosen[:, :, EXPERTS:EXPERTS + 1], 0.0).then_inc(chosen_done, 1)
                nc.vector.tensor_tensor(r1[:, 4, :], r1[:, 1, :], r1[:, 0, :], ALU.subtract).then_inc(gate_exp_in, 1)
                dve.wait_ge(gate_exp, 1)
                link(nc.vector.tensor_scalar(r1[:, 6, :], r1[:, 5, :], 1.0, None, ALU.add))
                link(nc.vector.reciprocal(r1[:, 7, :], r1[:, 6, :]))
                link(nc.vector.tensor_tensor(r1[:, 3, :], r1[:, 5, :], r1[:, 7, :], ALU.mult))
                link(nc.vector.tensor_tensor(tmp, oh1, per_token(7), ALU.mult))
                link(nc.vector.tensor_tensor(first, oh2, per_token(3), ALU.mult))
                link(nc.vector.tensor_tensor(gates[:, :, 0:EXPERTS], tmp, first, ALU.add))
                dve.wait_ge(pos_done, 1)
                nc.vector.memset(pos[:, :, EXPERTS:EXPERTS + 1], 0.0)
                cnt = ps[:, 2, 0:TB * EXPERTS]
                link(nc.vector.tensor_copy(pos[:, :, 0:EXPERTS], cnt.rearrange("p (b e) -> p b e", b=TB)))
                make_pick(0, 0, 0)
                dve.wait_ge(counted, 1)
                link(nc.vector.tensor_reduce(full[:, 0:1], ps[:, 6, 0:EXPERTS], AX.X, ALU.max))
                link(nc.vector.tensor_scalar(full_i[:, :], full[:, 0:1], float(PASS_SLOTS), None, ALU.is_gt))
                nc.vector.memset(full[:, 1:2], 0.0).then_inc(routed, 1)

            def gathered_lo(it):
                for g in range(2):
                    dve.wait_ge(ga_hi, 2 * it + g + 1)
                    nc.vector.tensor_tensor(xT_lo[:, 4 * g:4 * g + 4, 0:P], bank(1 + 2 * g).rearrange("p (k s) -> p k s", s=P),
                                            xT_hi[:, 4 * g:4 * g + 4, 0:P].bitcast(F32), ALU.subtract).then_inc(ga_lo, 1)

            def accumulate(it, e):
                for g in range(2):
                    for b in range(TB):
                        dve.wait_ge(sct_done, 4 * it + 2 * g + b + 1)
                        if not (isinstance(it, int) and it == 0):
                            dve.wait_ge(x_acc, 4 * it)
                        cols = slice(512 * g, 512 * g + 512)
                        src = bank(6 + g) if b == 0 else bank(1 + 2 * g)
                        nc.vector.scalar_tensor_tensor(x[:, b, cols], src, gates[:, b, bass.ds(e, 1)], x[:, b, cols],
                                                       ALU.mult, ALU.add).then_inc(x_acc, 1)

            def expert_of(p):
                def expert(dve, it, first, last):
                    e = it - p * EXPERTS

                    def previous():
                        if not first:
                            accumulate(it - 1, e - 1)

                    def pick_next():
                        if not last:
                            dve.wait_ge(st_done, it + 1)
                            make_pick(it + 1, p, e + 1)

                    def gather_next():
                        if not last:
                            gathered_lo(it + 1)

                    ffn(MOE, EXPERT_STEPS * it, DENSE_UNITS + UNITS * it, 1, extra=previous, cut=last,
                        xtra_end=gather_next, mid=pick_next)
                    for g in range(2):
                        dve.wait_ge(y_hi_out, 2 * it + g + 1)
                        if g == 0 and not first:
                            dve.wait_ge(sct_done, 4 * it)
                        nc.vector.tensor_tensor(y_lo[g], bank(4 + g).rearrange("p (k s) -> p k s", s=P), y_hi[g].bitcast(F32),
                                                ALU.subtract).then_inc(y_lo_out, 1)
                return expert

            def renew(split_next):
                dve.wait_ge(y_half, 1)
                update(2, 0)
                transposed_lo(2, 0)
                multiplied(dve, FIRST_TILE["attn1"] - 1)
                update(2, 1)
                split_next(0)
                transposed_lo(2, 1)
                split_next(1)
                inverse_rms(2)

            dve.wait_ge(gain_in, 16)
            for h in range(2):
                dve.wait_ge(x_in[h], 16)
                for b in range(TB):
                    x_times_gain(0, h, b)
            transposed_lo(0, 0)
            split_lo(dve, 0)
            transposed_lo(0, 1)
            split_lo(dve, 1)
            split_lo(dve, 2)
            inverse_rms(0)
            dve.wait_ge(const_in, 16)
            attention(0)
            dve.wait_ge(norm_inv, 2)
            ffn(FIRST_TILE["ffn0"], 0, 0, TB, k_norm=1, ending=renew)
            dve.wait_ge(rw_hi, 1)
            nc.vector.tensor_tensor(wr_parts[:, :, 1, :], wr[:, :, :], wr_parts[:, :, 0, :].bitcast(F32), ALU.subtract).then_inc(rw_lo, 1)
            attention(1)
            dve.wait_ge(norm_inv, 4)
            route()
            dve.wait_ge(routed, 1)
            gathered_lo(0)
            passes(expert_of(0), dve, 0)
            accumulate(EXPERTS - 1, EXPERTS - 1)
            dve.wait_ge(x_acc, 4 * EXPERTS)
            more = dve.value_load(full_i[0:1, 0:1], min_val=0, max_val=1)
            with dve.If(more == 1):
                nc.vector.tensor_scalar(pos[:, :, :], pos[:, :, :], -float(PASS_SLOTS), None, ALU.add).then_inc(pos_moved, 1)
                dve.wait_ge(pos_moved, 1)
                for n in range(LEAD):
                    split_lo(dve, MOE + n, EXPERT_STEPS * EXPERTS)
                make_pick(EXPERTS, 1, 0)
                gathered_lo(EXPERTS)
                passes(expert_of(1), dve, 1)
                accumulate(2 * EXPERTS - 1, EXPERTS - 1)
                dve.wait_ge(x_acc, 8 * EXPERTS)
            dve.wait_ge(gain_in, 16 * NORMS)

            def last_gain():
                nc.vector.tensor_tensor(xn[:, 1, :], x[:, 1, :], gain[:, :], ALU.mult).then_inc(xg_last, 1)

            inverse_rms(4, meanwhile=last_gain)
            dve.wait_ge(norm_inv, 5)
            nc.vector.scalar_tensor_tensor(xn[:, 0, :], x[:, 0, :], n_inv[:, 4, 0:1], gain[:, :], ALU.mult, ALU.mult).then_inc(xn_out0, 1)

        @block.tensor
        def _(pe):
            def tile_ready(n, step=0):
                pe.wait_ge(lo_ready, n + 1 + UNIT_TILES * step)

            def transpose_x(k, h):
                for b in range(TB):
                    pe.wait_ge(xg_ready, 4 * k + TB * h + b + 1)
                    for g in (2 * h, 2 * h + 1):
                        for c in range(2):
                            last = nc.tensor.transpose(ps[:, 4 * (k % 2) + g, c * SEQ + b * P:c * SEQ + (b + 1) * P],
                                                       xn[:, b, (2 * g + c) * P:(2 * g + c + 1) * P], ident)
                        if b == TB - 1:
                            last.then_inc(tr_done, 1)

            def multiply(n, step, cols, acts, k0, outs, first, last, between=None, first_block=None):
                tile_ready(n, step)
                hi, lo = hi_of(n, cols), lo_of(n, cols)
                K = hi.shape[1]
                for b, o in enumerate(outs):
                    if b == 1 and between:
                        between()
                    for k in range(K):
                        ins = product(o, acts[0][:, k0 + k, tok[b]], acts[1][:, k0 + k, tok[b]], hi[:, k, :], lo[:, k, :],
                                      first and k == 0, last and k == K - 1)
                    if b == 0 and first_block is not None:
                        ins.then_inc(first_block, 1)
                ins.then_inc(used, 1)

            xT = (xT_hi, xT_lo)
            uT = (uT_hi, uT_lo)

            def attention(layer):
                n = FIRST_TILE[f"attn{layer}"]
                k_norm = 2 * layer

                def transpose_latents():
                    pe.wait_ge(lat_ready, 4 * (layer + 1))
                    for g in range(3):
                        for c in range(2 * g, min(2 * g + 2, LC)):
                            for b in range(TB):
                                last = nc.tensor.transpose(ps[:, g, (c % 2) * SEQ + b * P:(c % 2) * SEQ + (b + 1) * P],
                                                           z[:, b, c * P:(c + 1) * P], ident)
                        last.then_inc(lt_done, 1)

                for g in range(N_IN + 1):
                    w = 512 if g < N_IN else REST
                    halves = 2 if g < N_IN else 1
                    if g >= 2:
                        pe.wait_ge(z_out, 10 * layer + 2 * (g - 1))
                    outs = [bank(4 + 2 * (g % 2) + b, w) for b in range(TB)]
                    for half in range(halves):
                        if g == 0:
                            pe.wait_ge(tr_lo, 4 * k_norm + 2 * (half + 1))
                        early = g == 0 and half == 0 and k_norm
                        multiply(n, 0, w, xT, 4 * half, outs, half == 0, half == halves - 1,
                                 between=(lambda: transpose_x(k_norm, 1)) if early else None)
                        n += 1
                        if (g, half) == (N_IN - 1, 0):
                            transpose_latents()
                def head_step(s):
                    i = HEAD_STEPS * layer + s
                    if s < HEAD_STEPS:
                        ca, h = HEAD_ORDER[s]
                        if s == HEADS:
                            pe.wait_ge(q_roped, 2 * TB * (layer + 1))
                            pe.wait_ge(k_roped, 2 * (layer + 1))
                            pe.wait_ge(kv_out, 4 * (layer + 1))
                        if s == 0:
                            pe.wait_ge(z_out, 10 * layer + 2 * N_IN)
                    if s < HEAD_STEPS and starts_turn(s):
                        g = turn_of(i)
                        if g >= 2:
                            pe.wait_ge(qk_out, g - 1)
                        d = P if ca else QK_MLA
                        for b in range(TB):
                            if ca:
                                q, k = z[:, b, CA_Q + h * HD:CA_Q + h * HD + P], z[:, b, CA_K + h * HD:CA_K + h * HD + P]
                            else:
                                q, k = q_mla[:, b, h * d:(h + 1) * d], k_mla[:, b, h, :]
                            nc.tensor.transpose(ps[0:d, g % 2, b * P:(b + 1) * P], q, ident)
                            last = nc.tensor.transpose(ps[0:d, g % 2, SEQ + b * P:SEQ + (b + 1) * P], k, ident)
                        last.then_inc(qk_done, 1)
                    if 1 <= s < HEAD_STEPS + 1:
                        j = i - 1
                        ca, h = HEAD_ORDER[s - 1]
                        first_row = HD * (h % 2) if ca else 0
                        pe.wait_ge(qk_out, turn_of(j) + 1)
                        if j >= 2:
                            pe.wait_ge(sc_out, j - 1)
                        qk = qkT[first_row:first_row + head_dims(ca), turn_of(j) % 2, :]
                        nc.tensor.matmul(ps[:, 2 + j % 2, 0:P], qk[:, 0:P], qk[:, SEQ:SEQ + P], start=True, stop=True)
                        nc.tensor.matmul(ps[:, 2 + j % 2, P:SCORES], qk[:, P:SEQ], qk[:, SEQ:2 * SEQ], start=True, stop=True).then_inc(sc_done, 1)
                    if s >= 4:
                        j = i - 4
                        ca, h = HEAD_ORDER[s - 4]
                        pe.wait_ge(pT_out, j + 1)
                        if j >= 4 and h % 2 == 0:
                            pe.wait_ge(o_lo, j // 2 - 1)
                        if s < 6:
                            pe.wait_ge(kv_out, 4 * layer + s - 1)
                        o = ps[HD * (h % 2):HD * (h % 2) + HD, 6 + j // 2 % 2, :]
                        v = (z[:, :, CA_V:CA_V + CA] if ca else v_mla[:, :, :])[:, :, HD * h:HD * (h + 1)]
                        nc.tensor.matmul(o[:, 0:SEQ], v[:, 0, :], pT[:, j % 2, 0:SEQ], start=True, stop=False)
                        nc.tensor.matmul(o[:, P:SEQ], v[:, 1, :], pT[:, j % 2, SEQ:SCORES], start=False, stop=True).then_inc(o_done, 1)
                    if 3 <= s < HEAD_STEPS + 3:
                        j = i - 3
                        pe.wait_ge(p_ready, j + 1)
                        if s < 5:
                            pe.wait_ge(kv_out, 4 * layer + s - 2)
                        if j >= 2:
                            pe.wait_ge(pT_out, j - 1)
                        for c in range(3):
                            last = nc.tensor.transpose(ps[:, 4 + j % 2, c * P:(c + 1) * P], s_sb[:, j % 3, c * P:(c + 1) * P], ident)
                        last.then_inc(pT_done, 1)
                    if s >= HEAD_STEPS:
                        if s == HEAD_STEPS:
                            tile_ready(n)
                            pe.wait_ge(o_lo, HEADS * layer + HEADS // 2)
                            pe.wait_ge(qk_out, TURNS * (layer + 1))
                        hi, lo = hi_of(n, 512), lo_of(n, 512)
                        part = s - HEAD_STEPS
                        for b in range(TB):
                            ins = product(bank(b), xT_hi[:, 4 + part, tok[b]], xT_lo[:, 4 + part, tok[b]],
                                          hi[:, part, :], lo[:, part, :], part == 0, False)
                        if part == 3:
                            ins.then_inc(used, 1)

                pe.wait_ge(lt_lo, 3 * (layer + 1))
                head_step(0)
                pe.wait_ge(z_out, 10 * (layer + 1))
                for j in range(2):
                    multiply(n, 0, Q_LORA, uT, 0, [bank(4 + 2 * j + b, Q_LORA) for b in range(TB)], True, True)
                    n += 1
                    head_step(j + 1)
                pe.wait_ge(q_out, 4 * (layer + 1))
                tile_ready(n)
                hi, lo = hi_of(n, 2 * CA), lo_of(n, 2 * CA)
                for g in range(2):
                    for b in range(TB):
                        for k in range(2):
                            ins = product(bank(4 + 2 * g + b), uT_hi[:, QC + k, tok[b]], uT_lo[:, QC + k, tok[b]],
                                          hi[:, k, 512 * g:512 * g + 512], lo[:, k, 512 * g:512 * g + 512], k == 0, k == 1)
                ins.then_inc(used, 1)
                n += 1
                for s in range(3, HEAD_STEPS + 4):
                    head_step(s)
                n += 1
                pe.wait_ge(o_lo, HEADS * (layer + 1))
                for g, half in W_OUT_ORDER[1:]:
                    first = half == W_OUT_ORDER[2 * g][1]
                    multiply(n, 0, 512, xT, 4 * half, [bank(2 * g + b) for b in range(TB)], first, not first,
                             first_block=w_out_first if (g, half) == (1, 1) else None)
                    n += 1
                    if (g, half) == (1, 0):
                        transpose_x(k_norm + 1, 0)

            def ffn(n, step, u0, blocks, extra=None, mid=None, xtra_end=None, y_wait=None, k_norm=None, gathered=None, by_columns=None):
                def up(n, st, first_bank, free, f):
                    if not _is_zero(u0, f):
                        pe.wait_ge(free, u0 + blocks * f)
                    start = k_norm is not None and isinstance(f, int) and f == 0 and first_bank == 0
                    for half in range(2):
                        if start:
                            pe.wait_ge(tr_lo, 4 * k_norm + 2 * (half + 1))
                        if gathered is not None and isinstance(f, int) and f == 0 and first_bank == 0:
                            pe.wait_ge(ga_lo, 2 * gathered + half + 1)
                        multiply(n + half, st, 512, xT, 4 * half, [bank(first_bank + b) for b in range(blocks)], half == 0, half == 1,
                                 between=(lambda: transpose_x(k_norm, 1)) if start and half == 0 else None)

                def transpose_hidden(f):
                    for b in range(blocks):
                        pe.wait_ge(hid_done, u0 + blocks * f + b + 1)
                        for k in range(4):
                            last = nc.tensor.transpose(ps[:, 2 + b, k * P:(k + 1) * P], hid[:, b, k * P:(k + 1) * P], ident)
                        last.then_inc(ht_done, 1)

                def down(n, st, f, first, last):
                    pe.wait_ge(ht_lo, u0 + blocks * (f + 1))
                    for half in range(2):
                        down_tile(n + half, st, half, first and half == 0, last and half == 1)

                def down_part(n, half, g, first, last):
                    hi, lo = hi_of(n, D), lo_of(n, D)
                    for b in range(blocks):
                        for k in range(2):
                            o = bank(4 + 2 * g + b) if blocks == TB else bank(4 + g)
                            ins = product(o, uT_hi[:, 2 * half + k, tok[b]], uT_lo[:, 2 * half + k, tok[b]],
                                          hi[:, k, 512 * g:512 * g + 512], lo[:, k, 512 * g:512 * g + 512],
                                          first and k == 0, last and k == 1)
                    return ins

                def down_tile(n, st, half, first, last):
                    tile_ready(n, st)
                    ins = down_part(n, half, 0, first, last)
                    if last:
                        ins.then_inc(y_half, 1)
                    down_part(n, half, 1, first, last).then_inc(used, 1)

                up(n, step, 0, silu_done, 0)
                up(n + 2, step, 2, ht_lo, 0)
                if extra:
                    extra()
                transpose_hidden(0)
                if y_wait:
                    y_wait()

                def unit(f, st, first):
                    up(n + 4, st, 0, silu_done, f)
                    up(n + 6, st, 2, ht_lo, f)
                    down(n + 8, st, f - 1, first, False)
                    transpose_hidden(f)

                unit(1, step, True)
                if mid:
                    mid()
                with pe.Fori(2, UNITS) as f:
                    unit(f, step + f - 1, False)
                if xtra_end:
                    xtra_end()
                if not by_columns:
                    down(n + 4, step + UNITS - 1, UNITS - 1, False, True)
                    return
                pe.wait_ge(ht_lo, u0 + blocks * UNITS)
                for g in range(2):
                    for half in range(2):
                        if g == 0:
                            tile_ready(n + 4 + half, step + UNITS - 1)
                        if (g, half) == (1, 1):
                            by_columns()
                        ins = down_part(n + 4 + half, half, g, False, half == 1)
                        if (g, half) == (0, 1):
                            ins.then_inc(y_half, 1)
                        if g == 1:
                            ins.then_inc(used, 1)

            def gather(it):
                pe.wait_ge(xn_ready, TB)
                pe.wait_ge(pick_done, it + 1)
                for c in range(DC):
                    for b in range(TB):
                        last = nc.tensor.matmul(ps[:, 1 + 2 * (c // 4), (c % 4) * P:(c % 4 + 1) * P], xn[:, b, c * P:(c + 1) * P],
                                                pick[:, b, :], start=(b == 0), stop=(b == TB - 1))
                    if c % 4 == 3:
                        last.then_inc(ga_done, 1)

            def scatter(it):
                pe.wait_ge(st_out, it + 1)
                for g in range(2):
                    pe.wait_ge(y_lo_out, 2 * it + g + 1)
                    for b in range(TB):
                        o = (bank(6 + g) if b == 0 else bank(1 + 2 * g)).rearrange("p (k s) -> p k s", s=P)
                        nc.tensor.matmul(o, pickT[:, b * P:(b + 1) * P], y_hi[g], start=True, stop=False)
                        nc.tensor.matmul(o, pickT[:, b * P:(b + 1) * P], y_lo[g], start=False, stop=True).then_inc(sct_done, 1)

            def expert(pe, it, first, last):
                def scatter_last():
                    if not first:
                        scatter(it - 1)

                def transpose_pick():
                    if not first:
                        pe.wait_ge(x_acc, 4 * it)
                    for b in range(TB):
                        ins = nc.tensor.transpose(ps[:, 6, b * P:(b + 1) * P], pick[:, b, :], ident)
                    ins.then_inc(st_done, 1)

                def gather_next():
                    if not last:
                        if not first:
                            pe.wait_ge(x_acc, 4 * it)
                        gather(it + 1)

                def y_free():
                    if not first:
                        pe.wait_ge(y_lo_out, 2 * it)

                ffn(MOE, EXPERT_STEPS * it, DENSE_UNITS + UNITS * it, 1, extra=scatter_last, mid=transpose_pick, xtra_end=gather_next, y_wait=y_free, gathered=it)
                if last:
                    scatter(it)

            pe.wait_ge(ident_in, 16)
            transpose_x(0, 0)
            transpose_x(0, 1)
            attention(0)
            ffn(FIRST_TILE["ffn0"], 0, 0, TB, k_norm=1, by_columns=lambda: transpose_x(2, 0))
            attention(1)
            def logits(h):
                for c in range(4 * h, 4 * h + 4):
                    pe.wait_ge(tr_lo, 12 + c // 2 + 1)
                    for b in range(TB):
                        for i, a in enumerate((xT_hi, xT_lo)):
                            ins = nc.tensor.matmul(bank(b, 2 * EXPERTS), a[:, c, tok[b]], wr_parts[:, c, :, :].rearrange("p i e -> p (i e)"),
                                                   start=(c == 0 and i == 0), stop=(c == DC - 1 and i == 1))
                return ins

            pe.wait_ge(rw_lo, 1)
            logits(0)
            transpose_x(3, 1)
            logits(1).then_inc(logit_done, 1)
            pe.wait_ge(const_in, 16)
            pe.wait_ge(chosen_done, 1)
            first, second = chosen[:, 0, 0:EXPERTS], chosen[:, 1, 0:EXPERTS]
            nc.tensor.matmul(ps[:, 2, 0:EXPERTS], tri, first, start=True, stop=True)
            nc.tensor.matmul(ps[:, 2, EXPERTS:2 * EXPERTS], ones, first, start=True, stop=False)
            nc.tensor.matmul(ps[:, 2, EXPERTS:2 * EXPERTS], tri, second, start=False, stop=True).then_inc(pos_done, 1)
            nc.tensor.matmul(ps[:, 6, 0:EXPERTS], ones, first, start=True, stop=False)
            nc.tensor.matmul(ps[:, 6, 0:EXPERTS], ones, second, start=False, stop=True).then_inc(counted, 1)
            gather(0)
            passes(expert, pe, 0)
            pe.wait_ge(routed, 1)
            more = pe.value_load(full_i[0:1, 0:1], min_val=0, max_val=1)
            with pe.If(more == 1):
                pe.wait_ge(x_acc, 4 * EXPERTS)
                gather(EXPERTS)
                passes(expert, pe, 1)


def _is_zero(u0, f):
    return isinstance(u0, int) and u0 == 0 and isinstance(f, int) and f == 0


def _constants():
    c = np.zeros((P, C_ALL), np.float32)
    c[:, C_ID:C_ID + P] = np.eye(P)
    for diagonal in (0, 2 * P):
        c[0:CHUNK, C_MASK + diagonal + CHUNK:C_MASK + diagonal + P] = NEG
    c[:, C_TRI:C_TRI + P] = np.triu(np.ones((P, P)), 1)
    c[:, C_ONE:C_ONE + P] = 1
    c[:, C_IOTA:C_IOTA + P] = np.arange(P)
    inv = (1.0 / (np.float32(10000.0) ** (np.arange(0, ROPE, 2, dtype=np.float32) / np.float32(ROPE)))).astype(np.float32)
    ang = np.arange(SEQ, dtype=np.float32)[:, None] * inv[None, :]
    for at, f in ((C_COS, np.cos), (C_SIN, np.sin)):
        c[:, at:at + TB * HALF] = f(ang).reshape(TB, P, HALF).transpose(1, 0, 2).reshape(P, TB * HALF)
    return c


_INS = ["x", "attn_norm", "w_in", "q_norm", "w_uq", "kv_norm", "w_ukv", "w_out", "ffn_norm",
        "dense_w1", "dense_w3", "dense_w2", "w_router", "moe_w1", "moe_w3", "moe_w2"]


def kernel(**inputs):
    import concourse.bacc as _bacc
    from concourse.bass_utils import run_bass_kernel_spmd as _run

    nc = _bacc.Bacc("TRN2", target_bir_lowering=False, num_devices=1)
    arrays = {n: np.ascontiguousarray(inputs[n]) for n in _INS}
    arrays["final_norm"] = np.ascontiguousarray(inputs["final_norm"]).reshape(1, D)
    arrays["rel_rev"] = np.ascontiguousarray(np.asarray(inputs["rel_bias"])[:, :, ::-1]).reshape(DEPTH * HEADS, 2 * REL + 1)
    arrays["const"] = _constants()
    t = {n: nc.dram_tensor(f"in_{n}", a.shape, mybir.dt.from_np(a.dtype), kind="ExternalInput").ap() for n, a in arrays.items()}
    out = nc.dram_tensor("out_y", (1, SEQ, D), F32, kind="ExternalOutput").ap()
    build(nc, t, out)
    r = _run(nc, [{f"in_{n}": a for n, a in arrays.items()}], core_ids=[0])
    return r.results[0]["out_y"]
```
